# Optimizing a Trainium2 kernel written in Bass

```python
import math
import jax, jax.numpy as jnp
from jax import lax
import numpy as np

D_MODEL = 1024
BATCH = 1
SEQ = 1024
DEPTH = 1

HEAD_DIM = 64
N_Q_HEADS = 8
N_KV_HEADS = 2
Q_PER_KV = N_Q_HEADS // N_KV_HEADS
ATTN_WIDTH = N_Q_HEADS * HEAD_DIM
KV_WIDTH = N_KV_HEADS * HEAD_DIM
WINDOW = 128
BLOCK = 128
N_BUCKETS = 32
MAX_DISTANCE = 128
CONV_WIDTH = D_MODEL - ATTN_WIDTH
CONV_GROUPS = 8
CONV_K = 3
IN_PROJ_WIDTH = ATTN_WIDTH + 2 * KV_WIDTH + 3 * CONV_WIDTH
D_FF = -(-8 * D_MODEL // (3 * 256)) * 256
N_MOD = 6
EPS = 1e-6
NEG_INF = -1e30

kernel_name = "hymba_swa_sink_shortconv_adaln_block"

def rmsnorm(x, g):
    xf = x.astype(jnp.float32)
    y = xf * lax.rsqrt(jnp.mean(xf * xf, axis=-1, keepdims=True) + EPS)
    return (y * g.astype(jnp.float32)).astype(x.dtype)

def t5_bucket(dist):
    max_exact = N_BUCKETS // 2
    is_small = dist < max_exact
    d = jnp.maximum(dist, 1).astype(jnp.float32)
    large = max_exact + (jnp.log(d / max_exact) / math.log(MAX_DISTANCE / max_exact)
                         * (N_BUCKETS - max_exact)).astype(jnp.int32)
    large = jnp.minimum(large, N_BUCKETS - 1)
    return jnp.where(is_small, dist, large)

def banded_sink_attention(q, k, v, sinks, rel_bias):
    b, s = q.shape[0], q.shape[1]
    nb = s // BLOCK
    qb = q.reshape(b, nb, BLOCK, N_KV_HEADS, Q_PER_KV, HEAD_DIM)
    kb = k.reshape(b, nb, BLOCK, N_KV_HEADS, HEAD_DIM)
    vb = v.reshape(b, nb, BLOCK, N_KV_HEADS, HEAD_DIM)

    def with_prev(t):
        prev = jnp.concatenate([jnp.zeros_like(t[:, :1]), t[:, :-1]], axis=1)
        return jnp.concatenate([prev, t], axis=2)

    kw, vw = with_prev(kb), with_prev(vb)
    scores = jnp.einsum("bnqkgd,bnskd->bnkgqs", qb, kw).astype(jnp.float32) * (HEAD_DIM ** -0.5)

    qi = jnp.arange(BLOCK, dtype=jnp.int32)[:, None]
    sj = jnp.arange(2 * BLOCK, dtype=jnp.int32)[None, :]
    dist = qi + BLOCK - sj
    bias = rel_bias[t5_bucket(jnp.maximum(dist, 0))]
    bias = jnp.transpose(bias, (2, 0, 1)).reshape(N_KV_HEADS, Q_PER_KV, BLOCK, 2 * BLOCK)
    scores = scores + bias.astype(jnp.float32)

    in_window = (dist >= 0) & (dist < WINDOW)
    key_pos = jnp.arange(nb, dtype=jnp.int32)[:, None] * BLOCK - BLOCK + sj
    valid = in_window[None] & (key_pos >= 0)[:, None, :]
    scores = jnp.where(valid[None, :, None, None], scores, NEG_INF)

    sink = sinks.astype(jnp.float32).reshape(N_KV_HEADS, Q_PER_KV)[None, None, :, :, None, None]
    m = jnp.maximum(jnp.max(scores, axis=-1, keepdims=True), sink)
    p = jnp.exp(scores - m)
    p = p / (jnp.sum(p, axis=-1, keepdims=True) + jnp.exp(sink - m))
    out = jnp.einsum("bnkgqs,bnskd->bnqkgd", p.astype(v.dtype), vw)
    return out.reshape(b, s, ATTN_WIDTH)

def causal_short_conv(u, w):
    s = u.shape[1]
    up = jnp.pad(u, ((0, 0), (CONV_K - 1, 0), (0, 0)))
    return w[0] * up[:, 0:s] + w[1] * up[:, 1:s + 1] + w[2] * up[:, 2:s + 2]

def setup_inputs(seed: int = 0) -> dict:
    key = jax.random.key(seed)
    ks = jax.random.split(key, 20)
    f32 = jnp.float32
    n = lambda k, shape, scale: (jax.random.normal(k, shape, f32) * scale)
    return {
        "x": n(ks[0], (BATCH, SEQ, D_MODEL), 1.0),
        "c": n(ks[1], (BATCH, D_MODEL), 1.0),
        "rel_bias": n(ks[2], (N_BUCKETS, N_Q_HEADS), 0.5),
        "w_ada": n(ks[3], (DEPTH, D_MODEL, N_MOD * D_MODEL), D_MODEL ** -0.5),
        "b_ada": n(ks[4], (DEPTH, N_MOD * D_MODEL), 0.01),
        "g_norm1": 1.0 + n(ks[5], (DEPTH, D_MODEL), 0.02),
        "w_in": n(ks[6], (DEPTH, D_MODEL, IN_PROJ_WIDTH), D_MODEL ** -0.5),
        "sinks": n(ks[7], (DEPTH, N_Q_HEADS), 1.0),
        "conv_w": n(ks[8], (DEPTH, CONV_K, CONV_WIDTH), CONV_K ** -0.5),
        "g_attn_out": 1.0 + n(ks[9], (DEPTH, ATTN_WIDTH), 0.02),
        "g_conv_out": 1.0 + n(ks[10], (DEPTH, CONV_WIDTH), 0.02),
        "w_out": n(ks[11], (DEPTH, D_MODEL, D_MODEL), D_MODEL ** -0.5),
        "g_norm2": 1.0 + n(ks[12], (DEPTH, D_MODEL), 0.02),
        "w_gu": n(ks[13], (DEPTH, D_MODEL, 2 * D_FF), D_MODEL ** -0.5),
        "w_down": n(ks[14], (DEPTH, D_FF, D_MODEL), D_FF ** -0.5),
        "g_final": 1.0 + n(ks[15], (D_MODEL,), 0.02),
    }

def reference(x, c, rel_bias, w_ada, b_ada, g_norm1, w_in, sinks, conv_w, g_attn_out,
              g_conv_out, w_out, g_norm2, w_gu, w_down, g_final):
    b, s = x.shape[0], x.shape[1]
    cond = jax.nn.silu(c)
    splits = [ATTN_WIDTH, ATTN_WIDTH + KV_WIDTH, ATTN_WIDTH + 2 * KV_WIDTH,
              ATTN_WIDTH + 2 * KV_WIDTH + CONV_WIDTH, ATTN_WIDTH + 2 * KV_WIDTH + 2 * CONV_WIDTH]
    for l in range(DEPTH):
        mod = (cond @ w_ada[l] + b_ada[l])[:, None, :]
        sh1, sc1, g1, sh2, sc2, g2 = jnp.split(mod, N_MOD, axis=-1)

        h = rmsnorm(x, g_norm1[l]) * (1.0 + sc1) + sh1
        proj = h @ w_in[l]
        q, k, v, gate_b, gate_c, xc = jnp.split(proj, splits, axis=-1)
        q = q.reshape(b, s, N_Q_HEADS, HEAD_DIM)
        k = k.reshape(b, s, N_KV_HEADS, HEAD_DIM)
        v = v.reshape(b, s, N_KV_HEADS, HEAD_DIM)
        attn = banded_sink_attention(q, k, v, sinks[l], rel_bias)
        conv = gate_b * causal_short_conv(gate_c * xc, conv_w[l])
        merged = jnp.concatenate([rmsnorm(attn, g_attn_out[l]), rmsnorm(conv, g_conv_out[l])], axis=-1)
        x = x + g1 * (merged @ w_out[l])

        h2 = rmsnorm(x, g_norm2[l]) * (1.0 + sc2) + sh2
        gate, up = jnp.split(h2 @ w_gu[l], 2, axis=-1)
        x = x + g2 * ((jax.nn.silu(gate) * up) @ w_down[l])
    return rmsnorm(x, g_final)


_drawn_inputs = setup_inputs


def setup_inputs(seed=0):
    import zlib

    import numpy as np

    out = dict(_drawn_inputs(seed))
    spreads = {}
    factors = {'b_ada': 3.245,
     'g_norm1': 3.761,
     'sinks': 29.827,
     'g_attn_out': 69.672,
     'g_conv_out': 68.246,
     'g_norm2': 14.32,
     'g_final': 21.585}
    for name, (base, spread) in spreads.items():
        noise = np.random.default_rng([zlib.crc32(name.encode()), seed]).standard_normal(out[name].shape)
        drawn = base * np.exp(spread * noise) if base else spread * noise
        out[name] = __import__('jax').numpy.asarray(drawn.astype(out[name].dtype))
    for name, factor in factors.items():
        out[name] = (out[name] * factor).astype(out[name].dtype)
    return out
```

```python
from contextlib import ExitStack

import concourse.bass as bass
from concourse import mybir

P = 128
SEQ = 1024
D = 1024
HEAD = 64
HQ = 8
HKV = 2
G = HQ // HKV
ATTN = HQ * HEAD
KVW = HKV * HEAD
CONV = D - ATTN
TAPS = 3
WIDTH_IN = ATTN + 2 * KVW + 3 * CONV
FF = 2816
BUCKETS = 32
WINDOW = 128
MAX_DISTANCE = 128
EPS = 1e-6
MASKED = -1e30

KC = D // P
NT = SEQ // P
HALF = 512
QC = ATTN // P
CC = CONV // P
NQKV = QC + 2
SLOTS = 3
FG = FF // (2 * P)
DIAGS = 2 * WINDOW + P

V_COND, V_GN1, V_GAIN, V_TAPS = 0, KC, 2 * KC, 3 * KC
V_ROWS = V_TAPS + TAPS * CC

F32 = mybir.dt.float32
F32R = mybir.dt.float32r
I32 = mybir.dt.int32
ALU = mybir.AluOpType
ACT = mybir.ActivationFunctionType
AX = mybir.AxisListType

CONV_ORDER = list(range(QC, KC))
ATTN_ORDER = [2, 3, 0, 1]
WO_ORDER = CONV_ORDER + ATTN_ORDER


def hymba_layer(nc, x, c, rel_bias, w_ada, b_ada, g_norm1, w_in, sinks, conv_w, g_attn_out,
                g_conv_out, w_out, g_norm2, w_gu, w_down, g_final, bucket_table, out):
    ctx = ExitStack()
    with ctx:
        def sb(name, shape, dt=F32, stack=ctx):
            return stack.enter_context(nc.sbuf_tensor(name, shape, dt))

        def sem(name):
            return ctx.enter_context(nc.semaphore(name))

        h = sb("h", [P, 2, KC, SEQ], F32R)
        res = sb("res", [P, NT, KC, P])
        rows = sb("rows", [P, 4, D])
        ident = sb("ident", [P, P])
        ones = sb("ones", [P, P])
        vrow = sb("vrow", [V_ROWS, P])
        vcol = sb("vcol", [P, V_ROWS])
        cond = sb("cond", [P, KC])
        mod1 = sb("mod1", [P, 2 * KC])
        sumsq = sb("sumsq", [P, 2 * NT])
        inv = sb("inv", [P, 2 * NT])
        nwt = sb("nwt", [P, 3, 2 * NT])
        rtab = sb("rtab", [BUCKETS, HQ])
        sink = sb("sink", [P, HQ])
        nsink = sb("nsink", [P, HQ])
        negmax = sb("negmax", [P, 2, G])
        sinkarg = sb("sinkarg", [P, 2, G])
        psum_p = sb("psum_p", [P, 2, G])
        esink = sb("esink", [P, 2, G])
        den = sb("den", [P, G])
        rden = sb("rden", [P, G])

        with ExitStack() as fa:
            wi_raw = sb("wi_raw", [P, KC, P], F32, fa)
            wi = sb("wi", [P, SLOTS, 2, KC, P], F32R, fa)
            cbuf = sb("cbuf", [P, 2, SEQ], F32, fa)
            qkv = sb("qkv", [P, NQKV, SEQ], F32, fa)
            vtok = sb("vtok", [P, NT, KVW], F32, fa)
            bias = sb("bias", [P, HQ, 2 * P], F32, fa)
            s = sb("s", [P, 2, G, 2 * P], F32, fa)
            pT = sb("pT", [P, 2, G, 2, P], F32, fa)
            attn = sb("attn", [P, ATTN], F32, fa)
            qs = sb("qs", [P, QC, P], F32, fa)
            ks = sb("ks", [P, 2 * P], F32, fa)
        ada1_acc = cbuf[:, :, :].rearrange("p a n -> p (a n)")
        ada1_raw = qkv[:, 0:4, :].rearrange("p (a b) n -> p a (b n)", a=2)
        ada2_acc = cbuf[:, 0, :]
        btab = attn[0:BUCKETS, 0:DIAGS]
        diag = qs[0:HQ].rearrange("p c q -> p (c q)")[:, 0:DIAGS]

        with ExitStack() as fs:
            sb("skip_s", [P, (KC + SLOTS * 2 * KC) * P + 2 * SEQ + NQKV * SEQ], F32, fs)
            xT = sb("xT", [P, KC, SEQ], F32, fs)

        with ExitStack() as fb:
            stg = sb("stg", [P, 2, 2, KC, P], F32R, fb)
            htmp = sb("htmp", [P, D], F32, fb)
            wo = sb("wo", [P, 2, KC, D], F32R, fb)
            wo_raw = sb("wo_raw", [P, 2, D], F32, fb)

        with ExitStack() as fc:
            gu_raw = sb("gu_raw", [P, 2, 2, KC, P], F32, fc)
            gu = sb("gu", [P, 2, 2, 2, KC, P], F32R, fc)
            wd_raw = sb("wd_raw", [P, 2, D], F32, fc)
            wd = sb("wd", [P, 2, 2, D], F32R, fc)
            act = sb("act", [P, 2, 2, SEQ], F32R, fc)
            hid = sb("hid", [P, 2, HALF], F32, fc)

        ps = ctx.enter_context(nc.psum_tensor("ps", [P, 8, HALF], F32))
        ps_scores = ps[:, 2:4, :].rearrange("p b (g k) -> p (b g) k", g=2)
        ps_pT = ps[:, 4:6, :].rearrange("p b (g c q) -> p (b g) c q", g=2, c=2)
        ps_pv = ps[:, 6, 0:G * HEAD].rearrange("p (g d) -> p g d", g=G)
        ps_col = ps[:, 6, 256:256 + CC * NT].rearrange("p (i t) -> p i t", i=CC)
        ps_turn = ps[:, 7, :].rearrange("p (c q) -> p c q", c=QC)

        diag_dram = nc.dram_tensor("diag_dram", (HQ, P, DIAGS), F32, kind="Internal").ap()

        names = """vec_loaded bias_row_loaded table_loaded gn2_loaded
            ident_made const_made vec_turned vec_copied cond_made x_summed rms1_made x_scaled x_turned x_copied
            ada1_init ada1_added mod_summed mod_made
            h_full h_hi h_lo_v h_lo_g h_lo_done
            wi_loaded wi_hi wi_lo proj_done proj_copied xc_used b_used
            ada2_init ada2_init_row ada2_added ada2_summed ada2_made ada2_rows_set
            diag_summed diag_made diag_stored bias_loaded sink_neg
            v_turned v_copied
            q_staged scores_done scores_read max_ready probs_ready probs_turned probsT_copied pv_done pv_read
            attn_squared attn_turned attnT_copied
            conv_base conv_taps conv_squared conv_summed conv_sum_read
            wo_scaled wo_hi wo_lo rms_merged
            stg_hi stg_lo out_done x1_done x1_squared h2_scaled h2_shifted h2_turned h2_hi h2_lo
            gu_hi gu_lo wd_scaled wd_hi wd_lo gate_done up_done silu_done hid_done act_hi act_lo
            down_done res_added gf_loaded y_squared y_made stored""".split()
        S = {n: sem(n) for n in names}
        x_loaded = [sem(f"x_loaded{t}") for t in range(NT)]
        ada1_loaded = [sem(f"ada1_loaded{b}") for b in range(2)]
        ada2_loaded = [sem(f"ada2_loaded{b}") for b in range(4)]
        wo_loaded = [sem(f"wo_loaded{b}") for b in range(2)]
        xr_loaded = [sem(f"xr_loaded{b}") for b in range(2)]
        gu_loaded = [sem(f"gu_loaded{b}") for b in range(2)]
        wd_loaded = sem("wd_loaded")

        ADA2_RAW = [s[:, 0].rearrange("p g k -> p (g k)"), s[:, 1].rearrange("p g k -> p (g k)"),
                    pT[:, 0].rearrange("p g c q -> p (g c q)"), pT[:, 1].rearrange("p g c q -> p (g c q)")]

        x_t = x.rearrange("(t p) d -> t p d", p=P)
        out_t = out.rearrange("(t p) d -> t p d", p=P)
        w_in_v = w_in.rearrange("(k p) n -> p k n", p=P)
        w_ada_v = w_ada.rearrange("(k p) n -> k p n", p=P)
        w_out_v = w_out.rearrange("(k p) n -> k p n", p=P)
        w_gu_v = w_gu.rearrange("(k p) (s n) -> p s k n", p=P, s=2)
        w_down_v = w_down.rearrange("(g c p) n -> g p c n", c=2, p=P)

        def wi_loads(n):
            if n < QC:
                return [(wi_raw[:, :, u * HEAD:(u + 1) * HEAD],
                         w_in_v[:, :, (u * QC + n) * HEAD:(u * QC + n + 1) * HEAD]) for u in range(HKV)]
            return [(wi_raw[:, k:k + KC // 2, :], w_in_v[:, k:k + KC // 2, n * P:(n + 1) * P]) for k in (0, KC // 2)]

        def triple_loads(i, j):
            first = ATTN + 2 * KVW + (CONV, 2 * CONV, 0)[j]
            return [(wi_raw[:, k:k + KC // 2, :],
                     w_in_v[:, k:k + KC // 2, first:first + CONV][:, :, bass.ds(i * P, P)]) for k in (0, KC // 2)]

        block = ctx.enter_context(nc.Block())

        @block.sync
        def _(sp):
            for rows_of, first, n in ((c, V_COND, KC), (g_norm1, V_GN1, KC), (g_attn_out, V_GAIN, QC),
                                      (g_conv_out, V_GAIN + QC, CC)):
                sp.dma_start(vrow[first:first + n, :],
                             rows_of.rearrange("(r p) -> r p", p=P)).then_inc(S["vec_loaded"], 16)
            sp.dma_start(vrow[V_TAPS:V_ROWS, :],
                         conv_w.rearrange("j (r p) -> (j r) p", p=P)).then_inc(S["vec_loaded"], 16)
            sp.wait_ge(S["ada1_init"], 1)
            sp.dma_start(ada1_acc[0:1, :], b_ada[0:2 * D].rearrange("(a n) -> a n", a=1)).then_inc(S["bias_row_loaded"], 16)
            for t in range(NT):
                sp.dma_start(res[:, t, :, :].rearrange("p k n -> p (k n)"), x_t[t]).then_inc(x_loaded[t], 16)
            for k in range(KC):
                if k >= 2:
                    sp.wait_ge(S["ada1_added"], k - 1)
                sp.dma_start(ada1_raw[:, k % 2, :], w_ada_v[k, :, 0:2 * D]).then_inc(ada1_loaded[k % 2], 16)
            def load_wi(n, loads):
                if not (isinstance(n, int) and n == 0):
                    sp.wait_ge(S["wi_hi"], n)
                    sp.wait_ge(S["wi_lo"], n)
                for dst, src in loads:
                    sp.dma_start(dst, src).then_inc(S["wi_loaded"], 16)

            for n in range(SLOTS):
                load_wi(n, wi_loads(n))
            sp.wait_ge(S["h_lo_done"], 1)
            sp.dma_start(rtab[:], rel_bias).then_inc(S["table_loaded"], 16)
            sp.dma_start(btab, bucket_table[0:BUCKETS, :]).then_inc(S["table_loaded"], 16)
            sp.dma_start(diag, bucket_table[BUCKETS:BUCKETS + HQ, :]).then_inc(S["table_loaded"], 16)
            sp.dma_start(sink[:], sinks.rearrange("(a n) -> a n", a=1).broadcast_to([P, HQ])).then_inc(S["table_loaded"], 16)
            sp.wait_ge(S["ada2_rows_set"], 1)
            sp.dma_start(rows[:, 2, :], g_norm2.rearrange("(a n) -> a n", a=1).broadcast_to([P, D])).then_inc(S["gn2_loaded"], 16)

            def ada2_loads(v):
                sp.wait_ge(S["ada2_init"], v + 1)
                sp.dma_start(ada2_acc[0:1, :], b_ada.rearrange("(a n) -> a n", a=1)[:, (2 + v) * D:(3 + v) * D]).then_inc(S["ada2_init_row"], 16)
                for k in range(KC):
                    if v == 0 and k < 4:
                        sp.wait_ge(S["h_lo_done"], 1)
                    else:
                        sp.wait_ge(S["ada2_added"], KC * v + k - 3)
                    sp.dma_start(ADA2_RAW[k % 4], w_ada_v[k, :, (2 + v) * D:(3 + v) * D]).then_inc(ada2_loaded[k % 4], 16)

            order = [("a", 0), ("w", 3), ("a", 1), ("w", 4), ("w", 5), ("a", 2), ("w", 6), ("a", 3), ("w", 7), ("w", 8)]
            for kind, n in order:
                if kind == "a":
                    ada2_loads(n)
                elif n < NQKV:
                    load_wi(n, wi_loads(n))
                else:
                    load_wi(n, triple_loads(0, n - NQKV))
                if (kind, n) == ("a", 0):
                    sp.wait_ge(S["diag_made"], 1)
                    sp.dma_start(diag_dram, diag.rearrange("h (a k) -> h a k", a=1).broadcast_to([HQ, P, DIAGS])).then_inc(S["diag_stored"], 16)
                    sp.wait_ge(S["diag_stored"], 16)
                    sp.dma_start(bias[:], bass.AP(tensor=diag_dram.tensor, offset=P - 1,
                                                  ap=[[DIAGS - 1, P], [P * DIAGS, HQ], [1, 2 * P]])).then_inc(S["bias_loaded"], 16)

            with sp.Fori(0, CC - 1) as i:
                for j in range(3):
                    load_wi(NQKV + 3 + i * 3 + j, triple_loads(i + 1, j))

            sp.wait_ge(S["attnT_copied"], NT)
            sp.wait_ge(S["conv_summed"], CC)
            sp.wait_ge(S["proj_done"], 2 * (NQKV + 3 * CC))
            for n, k in enumerate(WO_ORDER):
                if n >= 2:
                    sp.wait_ge(S["wo_hi"], n - 1)
                    sp.wait_ge(S["wo_lo"], n - 1)
                sp.dma_start(wo_raw[:, n % 2, :], w_out_v[k]).then_inc(wo_loaded[n % 2], 16)

            def reload_x(t, par):
                sp.wait_ge(S["stg_hi"], t + 1)
                sp.wait_ge(S["stg_lo"], t + 1)
                sp.dma_start(res[:, bass.ds(t, 1), :, :].rearrange("p a k n -> p (a k n)"),
                             x[bass.ds(t * P, P), :]).then_inc(xr_loaded[par], 16)

            reload_x(0, 0)
            with sp.Fori(0, NT // 2 - 1) as i:
                reload_x(2 * i + 1, 1)
                reload_x(2 * i + 2, 0)
            reload_x(NT - 1, 1)

            sp.wait_ge(S["out_done"], 2 * NT)
            sp.wait_ge(S["h2_turned"], NT)
            sp.wait_ge(S["wo_lo"], KC)
            sp.dma_start(rows[:, 0, :], g_final.rearrange("(a n) -> a n", a=1).broadcast_to([P, D])).then_inc(S["gf_loaded"], 16)

            def load_gu(g, slot):
                for half in range(2):
                    sp.dma_start(gu_raw[:, slot, half, :, :],
                                 w_gu_v[:, half][:, :, bass.ds(g * 2 * P + slot * P, P)]).then_inc(gu_loaded[slot], 16)

            def load_wd(g):
                sp.dma_start(wd_raw[:], w_down_v[bass.ds(g, 1), :, :, :].rearrange("a p c n -> p (a c) n")).then_inc(wd_loaded, 16)

            load_gu(0, 0)
            load_gu(0, 1)
            load_wd(0)
            with sp.Fori(0, FG - 1) as g:
                for slot in range(2):
                    sp.wait_ge(S["gu_lo"], 2 * g + slot + 1)
                    load_gu(g + 1, slot)
                sp.wait_ge(S["wd_lo"], g + 1)
                load_wd(g + 1)

            for t in range(NT):
                sp.wait_ge(S["y_made"], t + 1)
                sp.dma_start(out_t[t], res[:, t, :, :].rearrange("p k n -> p (k n)")).then_inc(S["stored"], 16)
            sp.wait_ge(S["stored"], 16 * NT)

        @block.gpsimd
        def _(pool):
            pool.memset(ident[:], 0.0)
            pool.memset(ones[:], 1.0).then_inc(S["const_made"], 1)
            pool.drain()
            pool.affine_select(out=ident[:], in_=ident[:], compare_op=ALU.not_equal, fill=1.0, base=0,
                               pattern=[[-1, P]], channel_multiplier=1).then_inc(S["ident_made"], 1)
            for n, k in enumerate(range(2, KC, 3)):
                pool.wait_ge(S["h_hi"], k + 1)
                pool.tensor_tensor(h[:, 1, k, :], xT[:, k, :], h[:, 0, k, :], ALU.subtract).then_inc(S["h_lo_g"], 1)

            def stage_q(b, after):
                if after is not None:
                    pool.wait_ge(S["scores_done"], after)
                w = P if isinstance(b, int) and b == 0 else 2 * P
                pool.tensor_copy(ks[:, 2 * P - w:2 * P], qkv[:, QC, bass.ds((b + 1) * P - w, w)])
                pool.tensor_copy(qs[:], qkv[:, 0:QC, bass.ds(b * P, P)]).then_inc(S["q_staged"], 1)

            pool.wait_ge(S["proj_copied"], 2 * NQKV)
            pool.wait_ge(S["h_lo_done"], 1)
            stage_q(0, None)

            def body(i, first, last):
                stage_q(2 * i + 1, 4 * i + 2)
                pool.wait_ge(S["xc_used"], 2 * i + 2)
                if not first:
                    pool.wait_ge(S["conv_summed"], i)
                pool.tensor_tensor(cbuf[:, 1, :], cbuf[:, 0, :], vcol[:, bass.ds(V_TAPS + 2 * CC + i, 1)].broadcast_to([P, SEQ]),
                                   ALU.mult).then_inc(S["conv_base"], 1)
                if not last:
                    stage_q(2 * i + 2, 4 * i + 4)
                pool.wait_ge(S["b_used"], 2 * i + 2)
                y = res[:, :, bass.ds(QC + i, 1), :].rearrange("p t a n -> p t (a n)")
                pool.tensor_tensor(cbuf[:, 1, :].rearrange("p (t n) -> p t n", t=NT), y, y, ALU.mult).then_inc(S["conv_squared"], 1)

            body(0, True, False)
            with pool.Fori(1, CC - 1) as i:
                body(i, False, False)
            body(CC - 1, False, True)

            def stage_lo(t, par, after):
                pool.wait_ge(S["stg_hi"], t + 1)
                pool.tensor_tensor(stg[:, par, 1, :, :], res[:, bass.ds(t, 1), :, :].rearrange("p a k n -> p (a k) n"),
                                   stg[:, par, 0, :, :], ALU.subtract).then_inc(S["stg_lo"], 1)

            def shift(t):
                pool.wait_ge(S["h2_scaled"], t + 1)
                pool.tensor_tensor(htmp[:], htmp[:], rows[:, 1, :], ALU.add).then_inc(S["h2_shifted"], 1)

            stage_lo(0, 0, None)
            with pool.Fori(0, NT // 2 - 1) as i:
                stage_lo(2 * i + 1, 1, None)
                shift(2 * i)
                stage_lo(2 * i + 2, 0, None)
                shift(2 * i + 1)
            stage_lo(NT - 1, 1, None)
            shift(NT - 2)
            shift(NT - 1)

            with pool.Fori(0, FG) as g:
                pool.wait_ge(wd_loaded, 16 * g + 16)
                for cch in range(2):
                    ins = pool.tensor_tensor(wd_raw[:, cch, :], wd_raw[:, cch, :], rows[:, 3, :], ALU.mult)
                ins.then_inc(S["wd_scaled"], 1)

        @block.scalar
        def _(a):
            a.wait_ge(S["vec_copied"], 1)
            a.activation(cond[:], vcol[:, V_COND:V_COND + KC], ACT.Silu).then_inc(S["cond_made"], 1)
            for t in range(NT):
                a.wait_ge(x_loaded[t], 16)
                xt = res[:, t, :, :].rearrange("p k n -> p (k n)")
                a.activation(xT[:, 7 if t % 2 else 6, :], xt, ACT.Square, accum_out=sumsq[:, t:t + 1]).then_inc(S["x_summed"], 1)
                a.drain()
            for t in range(NT):
                a.wait_ge(S["x_turned"], t + 1)
                if t == 0:
                    a.drain()
                a.activation(xT[:, :, t * P:(t + 1) * P],
                             ps[:, 2 + 2 * (t % 2):4 + 2 * (t % 2), :].rearrange("p b (k n) -> p (b k) n", n=P),
                             ACT.Copy).then_inc(S["x_copied"], 1)

            def split_wi(n, slot):
                a.wait_ge(S["wi_loaded"], 32 * n + 32)
                if not (isinstance(n, int) and n < SLOTS):
                    a.wait_ge(S["proj_done"], 2 * (n - SLOTS + 1))
                a.activation(wi[:, slot, 0, :, :], wi_raw[:], ACT.Copy).then_inc(S["wi_hi"], 1)

            for n in range(SLOTS):
                split_wi(n, n)
            for k in range(KC):
                a.wait_ge(S["h_full"], k + 1)
                a.activation(h[:, 0, k, :], xT[:, k, :], ACT.Copy).then_inc(S["h_hi"], 1)

            with a.Fori(0, 2) as i:
                for j in range(3):
                    for half in range(2):
                        a.wait_ge(S["proj_done"], (3 * i + j) * 2 + half + 1)
                        a.activation(qkv[:, bass.ds(3 * i + j, 1), half * HALF:(half + 1) * HALF].rearrange("p a n -> p (a n)"),
                                     ps[:, half, :], ACT.Copy).then_inc(S["proj_copied"], 1)
                    split_wi(3 * i + j + SLOTS, j)
            a.wait_ge(S["v_turned"], 1)
            a.activation(vtok[:], ps[:, 4:6, :].rearrange("p b (t n) -> p (b t) n", n=P), ACT.Copy).then_inc(S["v_copied"], 1)
            a.wait_ge(S["max_ready"], 1)

            def exps(u, b, width):
                a.wait_ge(S["max_ready"], u + 1)
                for g in range(G):
                    a.activation(s[:, b, g, 2 * P - width:2 * P], s[:, b, g, 2 * P - width:2 * P], ACT.Exp,
                                 bias=negmax[:, b, g:g + 1], accum_out=psum_p[:, b, g:g + 1])
                a.activation(esink[:, b, :], sinkarg[:, b, :], ACT.Exp).then_inc(S["probs_ready"], 1)

            def copy_pT(u, b, width):
                a.wait_ge(S["probs_turned"], u + 1)
                cs = slice(2 - width // P, 2)
                a.activation(pT[:, b, :, cs, :], ps_pT[:, :, cs, :], ACT.Copy).then_inc(S["probsT_copied"], 1)

            def copy_c(i, half):
                a.wait_ge(S["proj_done"], 2 * (NQKV + 3 * i) + half + 1)
                if half == 0 and not (isinstance(i, int) and i == 0):
                    a.wait_ge(S["conv_taps"], i)
                a.activation(cbuf[:, 0, half * HALF:(half + 1) * HALF], ps[:, 0 + half, :], ACT.Copy).then_inc(S["proj_copied"], 1)

            def copy_attnT(b):
                a.wait_ge(S["attn_turned"], b + 1)
                a.activation(res[:, bass.ds(b, 1), 0:QC, :].rearrange("p a c q -> p (a c) q"), ps_turn, ACT.Copy).then_inc(S["attnT_copied"], 1)

            def square_attn(b, u):
                a.wait_ge(S["pv_read"], u + 1)
                a.activation(junk, attn[:], ACT.Square, accum_out=sumsq[:, bass.ds(b, 1)]).then_inc(S["attn_squared"], 1)
                a.drain()

            junk = ps[:, 7, :]

            def body(i, first, last):
                u, b = 4 * i, 2 * i
                w0 = P if first else 2 * P
                exps(u, 0, w0)
                copy_c(i, 0)
                copy_pT(u, 0, w0)
                exps(u + 1, 1, w0)
                copy_c(i, 1)
                copy_pT(u + 1, 1, w0)
                if not last:
                    split_wi(NQKV + 3 * i + 3, 0)
                exps(u + 2, 0, 2 * P)
                square_attn(b, u + 1)
                copy_pT(u + 2, 0, 2 * P)
                exps(u + 3, 1, 2 * P)
                copy_attnT(b)
                copy_pT(u + 3, 1, 2 * P)
                if not last:
                    split_wi(NQKV + 3 * i + 4, 1)
                square_attn(b + 1, u + 3)
                copy_attnT(b + 1)
                if not last:
                    split_wi(NQKV + 3 * i + 5, 2)

            body(0, True, False)
            with a.Fori(1, CC - 1) as i:
                body(i, False, False)
            body(CC - 1, False, True)

            def stage_hi(t, par):
                a.activation(stg[:, par, 0, :, :], res[:, bass.ds(t, 1), :, :].rearrange("p a k n -> p (a k) n"),
                             ACT.Copy).then_inc(S["stg_hi"], 1)

            a.drain()
            a.wait_ge(S["b_used"], 2 * CC)
            a.wait_ge(S["proj_done"], 2 * (NQKV + 3 * CC))
            stage_hi(0, 0)
            for n, k in enumerate(WO_ORDER):
                a.wait_ge(S["wo_scaled"], n + 1)
                if n == 0:
                    a.wait_ge(S["conv_summed"], CC)
                a.activation(wo[:, 0, k, :], wo_raw[:, n % 2, :], ACT.Copy).then_inc(S["wo_hi"], 1)

            def square_x1(t):
                a.wait_ge(S["x1_done"], 2 * t + 2)
                a.activation(ps[:, 6:8, :].rearrange("p b n -> p (b n)"), res[:, bass.ds(t, 1), :, :].rearrange("p a k n -> p (a k n)"), ACT.Square,
                             accum_out=sumsq[:, bass.ds(t, 1)]).then_inc(S["x1_squared"], 1)

            def h2_high(t):
                a.wait_ge(S["h2_turned"], t + 1)
                a.activation(h[:, 0, :, bass.ds(t * P, P)], ps[:, 4:6, :].rearrange("p b (k n) -> p (b k) n", n=P), ACT.Copy).then_inc(S["h2_hi"], 1)

            def restage(t, par):
                a.wait_ge(S["out_done"], 2 * (t - 1))
                stage_hi(t, par)

            stage_hi(1, 1)
            a.drain()
            with a.Fori(0, NT // 2 - 1) as i:
                square_x1(2 * i)
                a.drain()
                restage(2 * i + 2, 0)
                h2_high(2 * i)
                square_x1(2 * i + 1)
                a.drain()
                restage(2 * i + 3, 1)
                h2_high(2 * i + 1)
            square_x1(NT - 2)
            h2_high(NT - 2)
            a.drain()
            square_x1(NT - 1)
            h2_high(NT - 1)

            def split_gu(g, slot, first=False):
                a.wait_ge(gu_loaded[slot], 32 * g + 32)
                if not first:
                    a.wait_ge(S["up_done"], 4 * (g - 1) + 2 * slot + 2)
                a.activation(gu[:, slot, 0, :, :, :], gu_raw[:, slot, :, :, :], ACT.Copy).then_inc(S["gu_hi"], 1)

            def silu(n, half):
                a.wait_ge(S["gate_done"], 2 * n + half + 1)
                if not (isinstance(n, int) and n == 0):
                    a.wait_ge(S["act_lo"], 2 * n - 1 + half)
                a.activation(hid[:, half, :], ps[:, 2 * half, :], ACT.Silu).then_inc(S["silu_done"], 1)

            def act_high(n, slot, half):
                a.wait_ge(S["hid_done"], 2 * n + half + 1)
                a.activation(act[:, 0, slot, half * HALF:(half + 1) * HALF], hid[:, half, :], ACT.Copy).then_inc(S["act_hi"], 1)

            a.wait_ge(S["h2_lo"], NT)
            split_gu(0, 0, True)
            split_gu(0, 1, True)

            def ff(g, first, last):
                a.wait_ge(S["wd_scaled"], g + 1)
                if not first:
                    a.wait_ge(S["down_done"], 2 * NT * g)
                a.activation(wd[:, 0, :, :], wd_raw[:], ACT.Copy).then_inc(S["wd_hi"], 1)
                for slot in range(2):
                    for half in range(2):
                        silu(2 * g + slot, half)
                        act_high(2 * g + slot, slot, half)
                    if not last:
                        split_gu(g + 1, slot)

            ff(0, True, False)
            with a.Fori(1, FG - 1) as g:
                ff(g, False, False)
            ff(FG - 1, False, True)
            for t in range(NT):
                a.wait_ge(S["res_added"], 2 * NT * (FG - 1) + 2 * t + 2)
                if t == 0:
                    a.wait_ge(S["act_lo"], 4 * FG)
                a.activation(hid[:].rearrange("p b n -> p (b n)"), res[:, t, :, :].rearrange("p k n -> p (k n)"), ACT.Square,
                             accum_out=sumsq[:, t:t + 1]).then_inc(S["y_squared"], 1)
                a.drain()

        @block.vector
        def _(v):
            def inv_sqrt(dst, src, width, scale, done=None):
                m, y, w = nwt[:, 0, 0:width], nwt[:, 1, 0:width], nwt[:, 2, 0:width]
                v.tensor_scalar(m, src, scale, EPS, ALU.mult, ALU.add)
                v.drain()
                v.tensor_scalar(w.bitcast(I32), m.bitcast(I32), 1, None, ALU.logical_shift_right)
                v.drain()
                v.tensor_scalar(y.bitcast(I32), w.bitcast(I32), -1, 0x5F3759DF, ALU.mult, ALU.add)
                v.drain()
                for step in range(3):
                    v.tensor_tensor(w, m, y, ALU.mult)
                    v.drain()
                    v.scalar_tensor_tensor(w, w, -0.5, y, ALU.mult, ALU.mult)
                    v.drain()
                    ins = v.scalar_tensor_tensor(dst if step == 2 else y, w, 1.5, y, ALU.add, ALU.mult)
                    if step < 2:
                        v.drain()
                if done is not None:
                    ins.then_inc(done, 1)
                v.drain()

            v.memset(ada1_acc, 0.0).then_inc(S["ada1_init"], 1)
            for r in (0, 1, 3):
                ins = v.memset(rows[:, r, :], 1.0)
            ins.then_inc(S["ada2_rows_set"], 1)
            v.wait_ge(S["vec_turned"], 1)
            v.tensor_copy(vcol[:], ps[:, 6, 0:V_ROWS]).then_inc(S["vec_copied"], 1)
            for q in range(2):
                v.wait_ge(S["x_summed"], 4 * q + 4)
                inv_sqrt(inv[:, 4 * q:4 * q + 4], sumsq[:, 4 * q:4 * q + 4], 4, 1.0 / D)
                for t in range(4 * q, 4 * q + 4):
                    xt = res[:, t, :, :].rearrange("p k n -> p (k n)")
                    v.tensor_scalar(xt, xt, inv[:, t:t + 1], None, ALU.mult).then_inc(S["x_scaled"], 1)
            v.wait_ge(S["cond_made"], 1)
            v.wait_ge(S["bias_row_loaded"], 16)
            for k in range(KC):
                v.wait_ge(ada1_loaded[k % 2], 16 * (k // 2) + 16)
                v.scalar_tensor_tensor(ada1_acc, ada1_raw[:, k % 2, :], cond[:, k:k + 1], ada1_acc,
                                       ALU.mult, ALU.add).then_inc(S["ada1_added"], 1)
                v.drain()
            v.wait_ge(S["mod_summed"], 1)
            v.tensor_copy(mod1[:, 0:KC], ps[:, 7, 0:KC])
            v.scalar_tensor_tensor(mod1[:, KC:2 * KC], ps[:, 7, KC:2 * KC], 1.0, vcol[:, V_GN1:V_GN1 + KC],
                                   ALU.add, ALU.mult).then_inc(S["mod_made"], 1)
            v.drain()

            def wi_low(n, slot):
                v.wait_ge(S["wi_hi"], n + 1)
                v.tensor_tensor(wi[:, slot, 1, :, :], wi_raw[:], wi[:, slot, 0, :, :], ALU.subtract).then_inc(S["wi_lo"], 1)

            for n in range(SLOTS):
                wi_low(n, n)
            v.wait_ge(S["x_copied"], NT)

            def low(k):
                v.wait_ge(S["h_hi"], k + 1)
                v.tensor_tensor(h[:, 1, k, :], xT[:, k, :], h[:, 0, k, :], ALU.subtract).then_inc(S["h_lo_v"], 1)

            for k in range(KC):
                v.tensor_scalar(xT[:, k, :], xT[:, k, :], mod1[:, KC + k:KC + k + 1], mod1[:, k:k + 1],
                                ALU.mult, ALU.add).then_inc(S["h_full"], 1)
                if k >= 1 and (k - 1) % 3 != 2:
                    low(k - 1)
            if (KC - 1) % 3 != 2:
                low(KC - 1)
            v.drain()
            v.wait_ge(S["h_lo_g"], len(range(2, KC, 3)))
            v.memset(den[:], 1.0).then_inc(S["h_lo_done"], 1)

            v.wait_ge(S["diag_summed"], 1)
            v.tensor_tensor(diag, ps[0:HQ, 7, 0:DIAGS], diag, ALU.add).then_inc(S["diag_made"], 1)
            v.tensor_scalar(nsink[:], sink[:], -1.0, None, ALU.mult)

            def ada2(r):
                if not (isinstance(r, int) and r == 0):
                    v.wait_ge(S["ada2_summed"], r)
                v.memset(ada2_acc, 0.0).then_inc(S["ada2_init"], 1)
                v.wait_ge(S["ada2_init_row"], 16 * r + 16)
                for k in range(KC):
                    v.drain()
                    v.wait_ge(ada2_loaded[k % 4], 32 * r + 16 * (k // 4) + 16)
                    v.scalar_tensor_tensor(ada2_acc, ADA2_RAW[k % 4], cond[:, k:k + 1], ada2_acc,
                                           ALU.mult, ALU.add).then_inc(S["ada2_added"], 1)

            def ada2_row(r, first):
                v.wait_ge(S["ada2_summed"], r + 1)
                if first:
                    v.wait_ge(S["gn2_loaded"], 16)
                row = rows[:, r, :]
                v.scalar_tensor_tensor(row, ps[:, 6:8, :].rearrange("p b n -> p (b n)"), 1.0 if r == 2 else 0.0, row,
                                       ALU.add, ALU.mult).then_inc(S["ada2_made"], 1)

            for i in range(2):
                ada2(2 * i)
                wi_low(3 * i + 3, 0)
                ada2_row(2 * i, i == 0)
                ada2(2 * i + 1)
                wi_low(3 * i + 4, 1)
                wi_low(3 * i + 5, 2)
                ada2_row(2 * i + 1, False)
            v.drain()
            v.wait_ge(S["bias_loaded"], 16)

            def softmax_head(u, b, width, kv):
                cols = slice(2 * P - width, 2 * P)
                v.wait_ge(S["scores_done"], u + 1)
                if not (isinstance(u, int) and u < 2):
                    v.wait_ge(S["probs_turned"], u - 1)
                v.scalar_tensor_tensor(s[:, b, :, cols], ps_scores[:, :, cols], HEAD ** -0.5,
                                       bias[:, kv * G:(kv + 1) * G, cols], ALU.mult, ALU.add).then_inc(S["scores_read"], 1)
                v.drain()
                v.tensor_reduce(den[:], s[:, b, :, cols], AX.X, ALU.max)
                v.drain()
                v.scalar_tensor_tensor(negmax[:, b, :], den[:], -1.0, nsink[:, kv * G:(kv + 1) * G], ALU.mult, ALU.min)
                v.drain()
                v.tensor_tensor(sinkarg[:, b, :], negmax[:, b, :], sink[:, kv * G:(kv + 1) * G], ALU.add).then_inc(S["max_ready"], 1)

            def normalise(u, b, kv):
                v.wait_ge(S["probs_ready"], u + 1)
                v.tensor_tensor(rden[:], psum_p[:, b, :], esink[:, b, :], ALU.add)
                v.drain()
                v.reciprocal(rden[:], rden[:])
                v.drain()
                v.wait_ge(S["pv_done"], u + 1)
                v.tensor_tensor(attn[:, kv * G * HEAD:(kv + 1) * G * HEAD].rearrange("p (g d) -> p g d", g=G), ps_pv,
                                rden[:].rearrange("p (g a) -> p g a", a=1).broadcast_to([P, G, HEAD]),
                                ALU.mult).then_inc(S["pv_read"], 1)

            def gate_c(i, half):
                v.wait_ge(S["proj_done"], 2 * (NQKV + 3 * i + 1) + half + 1)
                v.wait_ge(S["proj_copied"], 2 * NQKV + 2 * i + half + 1)
                u = cbuf[:, 0, half * HALF:(half + 1) * HALF]
                v.tensor_tensor(u, ps[:, half, :], u, ALU.mult).then_inc(S["xc_used"], 1)

            def taps(i):
                v.wait_ge(S["conv_base"], i + 1)
                for lag in (1, 2):
                    if lag == 2:
                        v.drain()
                    y = cbuf[:, 1, lag:SEQ]
                    ins = v.scalar_tensor_tensor(y, cbuf[:, 0, 0:SEQ - lag], vcol[:, bass.ds(V_TAPS + (2 - lag) * CC + i, 1)], y,
                                                 ALU.mult, ALU.add)
                ins.then_inc(S["conv_taps"], 1)
                v.drain()

            def gate_b(i, half):
                v.wait_ge(S["proj_done"], 2 * (NQKV + 3 * i + 2) + half + 1)
                t0 = half * NT // 2
                v.tensor_tensor(res[:, t0:t0 + NT // 2, bass.ds(QC + i, 1), :].rearrange("p t a n -> p t (a n)"),
                                ps[:, half, :].rearrange("p (t n) -> p t n", n=P),
                                cbuf[:, 1, half * HALF:(half + 1) * HALF].rearrange("p (t n) -> p t n", n=P),
                                ALU.mult).then_inc(S["b_used"], 1)

            def body(i, first, last):
                u = 4 * i
                w0 = P if first else 2 * P
                softmax_head(u, 0, w0, 0)
                softmax_head(u + 1, 1, w0, 1)
                if not first:
                    v.wait_ge(S["attn_turned"], 2 * i)
                    v.wait_ge(S["attn_squared"], 2 * i)
                normalise(u, 0, 0)
                softmax_head(u + 2, 0, 2 * P, 0)
                if not last:
                    wi_low(NQKV + 3 * i + 3, 0)
                gate_c(i, 0)
                normalise(u + 1, 1, 1)
                softmax_head(u + 3, 1, 2 * P, 1)
                gate_c(i, 1)
                v.wait_ge(S["attn_turned"], 2 * i + 1)
                v.wait_ge(S["attn_squared"], 2 * i + 1)
                normalise(u + 2, 0, 0)
                taps(i)
                if not last:
                    wi_low(NQKV + 3 * i + 4, 1)
                gate_b(i, 0)
                normalise(u + 3, 1, 1)
                gate_b(i, 1)
                if not last:
                    wi_low(NQKV + 3 * i + 5, 2)

            body(0, True, False)
            with v.Fori(1, CC - 1) as i:
                body(i, False, False)
            body(CC - 1, False, True)

            v.wait_ge(S["conv_summed"], CC)
            v.tensor_reduce(sumsq[:, NT:2 * NT], ps_col.rearrange("p i t -> p t i"), AX.X, ALU.add).then_inc(S["conv_sum_read"], 1)
            v.drain()
            v.wait_ge(S["attn_squared"], NT)
            inv_sqrt(inv[:], sumsq[:], 2 * NT, 1.0 / ATTN, S["rms_merged"])
            for n, k in enumerate(WO_ORDER):
                v.wait_ge(wo_loaded[n % 2], 16 * (n // 2) + 16)
                raw = wo_raw[:, n % 2, :]
                v.scalar_tensor_tensor(raw, raw, vcol[:, V_GAIN + k:V_GAIN + k + 1], rows[:, 0, :], ALU.mult, ALU.mult).then_inc(S["wo_scaled"], 1)
                v.drain()
                v.wait_ge(S["wo_hi"], n + 1)
                v.tensor_tensor(wo[:, 1, k, :], raw, wo[:, 0, k, :], ALU.subtract).then_inc(S["wo_lo"], 1)

            def norm2(t, first):
                v.wait_ge(S["x1_squared"], t + 1)
                inv_sqrt(rden[:, 0:1], sumsq2(t), 1, 1.0 / D)
                if not first:
                    v.wait_ge(S["h2_turned"], t)
                v.scalar_tensor_tensor(htmp[:], res[:, bass.ds(t, 1), :, :].rearrange("p a k n -> p (a k n)"), rden[:, 0:1], rows[:, 2, :],
                                       ALU.mult, ALU.mult).then_inc(S["h2_scaled"], 1)

            def sumsq2(t):
                return sumsq[:, bass.ds(t, 1)]

            def h2_low(t):
                v.wait_ge(S["h2_hi"], t + 1)
                v.tensor_tensor(h[:, 1, :, bass.ds(t * P, P)], ps[:, 4:6, :].rearrange("p b (k n) -> p (b k) n", n=P),
                                h[:, 0, :, bass.ds(t * P, P)], ALU.subtract).then_inc(S["h2_lo"], 1)

            def add_pair(t, i, par):
                v.wait_ge(xr_loaded[par], 16 * i + 16)
                for half in range(2):
                    v.wait_ge(S["out_done"], 2 * t + half + 1)
                    r = res[:, bass.ds(t, 1), half * 4:half * 4 + 4, :].rearrange("p a k n -> p (a k n)")
                    v.scalar_tensor_tensor(r, ps[:, 2 * half, :], inv[:, bass.ds(NT + t, 1)], r, ALU.mult, ALU.add)
                    v.drain()
                    v.scalar_tensor_tensor(r, ps[:, 2 * half + 1, :], inv[:, bass.ds(t, 1)], r, ALU.mult, ALU.add).then_inc(S["x1_done"], 1)

            add_pair(0, 0, 0)
            norm2(0, True)
            with v.Fori(0, NT // 2 - 1) as i:
                add_pair(2 * i + 1, i, 1)
                h2_low(2 * i)
                norm2(2 * i + 1, False)
                add_pair(2 * i + 2, i + 1, 0)
                h2_low(2 * i + 1)
                norm2(2 * i + 2, False)
            add_pair(NT - 1, NT // 2 - 1, 1)
            h2_low(NT - 2)
            norm2(NT - 1, False)
            h2_low(NT - 1)

            def gu_low(g, slot):
                v.wait_ge(S["gu_hi"], 2 * g + slot + 1)
                v.tensor_tensor(gu[:, slot, 1, :, :, :], gu_raw[:, slot, :, :, :], gu[:, slot, 0, :, :, :],
                                ALU.subtract).then_inc(S["gu_lo"], 1)

            def times_up(n, slot, half):
                v.wait_ge(S["silu_done"], 2 * n + half + 1)
                v.wait_ge(S["up_done"], 2 * n + half + 1)
                v.tensor_tensor(hid[:, half, :], ps[:, 2 * half + 1, :], hid[:, half, :], ALU.mult).then_inc(S["hid_done"], 1)
                v.wait_ge(S["act_hi"], 2 * n + half + 1)
                v.tensor_tensor(act[:, 1, slot, half * HALF:(half + 1) * HALF], hid[:, half, :],
                                act[:, 0, slot, half * HALF:(half + 1) * HALF], ALU.subtract).then_inc(S["act_lo"], 1)

            def add_down(g, t, half):
                m = 2 * t + half
                v.wait_ge(S["down_done"], 2 * NT * g + m + 1)
                r = res[:, t, half * 4:half * 4 + 4, :].rearrange("p k n -> p (k n)")
                v.tensor_tensor(r, ps[:, 4 + m % 4, :], r, ALU.add).then_inc(S["res_added"], 1)

            gu_low(0, 0)
            gu_low(0, 1)

            def ff(g, last):
                v.wait_ge(S["wd_hi"], g + 1)
                v.tensor_tensor(wd[:, 1, :, :], wd_raw[:], wd[:, 0, :, :], ALU.subtract).then_inc(S["wd_lo"], 1)
                for slot in range(2):
                    for half in range(2):
                        times_up(2 * g + slot, slot, half)
                    if slot == 0 and not last:
                        gu_low(g + 1, 0)
                for t in range(NT):
                    for half in range(2):
                        add_down(g, t, half)
                    if t == 2 and not last:
                        gu_low(g + 1, 1)

            with v.Fori(0, FG - 1) as g:
                ff(g, False)
            ff(FG - 1, True)
            v.wait_ge(S["gf_loaded"], 16)
            for q in range(2):
                v.drain()
                v.wait_ge(S["y_squared"], 4 * q + 4)
                inv_sqrt(inv[:, 4 * q:4 * q + 4], sumsq[:, 4 * q:4 * q + 4], 4, 1.0 / D)
                for t in range(4 * q, 4 * q + 4):
                    r = res[:, t, :, :].rearrange("p k n -> p (k n)")
                    v.scalar_tensor_tensor(r, r, inv[:, t:t + 1], rows[:, 0, :], ALU.mult, ALU.mult).then_inc(S["y_made"], 1)

        @block.tensor
        def _(pe):
            def product(o, lhs, rhs, ks, first, last):
                ins = None
                for n, k in enumerate(ks):
                    for m, (a_, b_) in enumerate(((0, 0), (0, 1), (1, 0))):
                        ins = pe.matmul(o, lhs(a_, k), rhs(b_, k), start=first and n == 0 and m == 0,
                                        stop=last and n == len(ks) - 1 and m == 2)
                return ins

            pe.wait_ge(S["vec_loaded"], 80)
            pe.wait_ge(S["ident_made"], 1)
            pe.transpose(ps[:, 6, 0:V_ROWS], vrow[:], ident[0:V_ROWS, 0:V_ROWS]).then_inc(S["vec_turned"], 1)
            for t in range(NT):
                pe.wait_ge(S["x_scaled"], t + 1)
                if t >= 2:
                    pe.wait_ge(S["x_copied"], t - 1)
                for k in range(KC):
                    ins = pe.transpose(ps[:, 2 + 2 * (t % 2) + k // 4, (k % 4) * P:(k % 4 + 1) * P], res[:, t, k, :], ident[:])
                ins.then_inc(S["x_turned"], 1)
            pe.wait_ge(S["const_made"], 1)
            pe.wait_ge(S["ada1_added"], KC)
            for n in range(2 * KC):
                ins = pe.matmul(ps[:, 7, n:n + 1], ada1_acc[:, n * P:(n + 1) * P], ones[:, 0:1], start=True, stop=True)
            ins.then_inc(S["mod_summed"], 1)

            def project(n, slot, half, order_ready=False):
                o = ps[:, half, :]
                ins = product(o, lambda a_, k: wi[:, slot, a_, k, :],
                              lambda b_, k: h[:, b_, k, half * HALF:(half + 1) * HALF], range(KC), True, True)
                ins.then_inc(S["proj_done"], 1)

            pe.wait_ge(S["wi_lo"], 1)
            nv = ng = 0
            for k in range(KC):
                if k % 3 == 2:
                    ng += 1
                    pe.wait_ge(S["h_lo_g"], ng)
                else:
                    nv += 1
                    pe.wait_ge(S["h_lo_v"], nv)
                for half in range(2):
                    ins = product(ps[:, half, :], lambda a_, k: wi[:, 0, a_, k, :],
                                  lambda b_, k: h[:, b_, k, half * HALF:(half + 1) * HALF], [k], k == 0, k == KC - 1)
                    if k == KC - 1:
                        ins.then_inc(S["proj_done"], 1)

            def ada2_sum(r):
                pe.wait_ge(S["ada2_added"], KC * (r + 1))
                if r == 0:
                    pe.wait_ge(S["diag_made"], 1)
                else:
                    pe.wait_ge(S["ada2_made"], r)
                for half in range(2):
                    ins = pe.matmul(ps[:, 6 + half, :], ones[:], ada2_acc[:, half * HALF:(half + 1) * HALF], start=True, stop=True)
                ins.then_inc(S["ada2_summed"], 1)

            pe.wait_ge(S["table_loaded"], 64)
            pe.wait_ge(S["mod_made"], 1)
            pe.matmul(ps[0:HQ, 7, 0:DIAGS], rtab[:], btab, start=True, stop=True).then_inc(S["diag_summed"], 1)
            for n in range(1, NQKV):
                pe.wait_ge(S["wi_lo"], n + 1)
                for half in range(2):
                    pe.wait_ge(S["proj_copied"], 2 * (n - 1) + half + 1)
                    project(n, n % SLOTS, half)
                if n in (2, 3, 4, 5):
                    ada2_sum(n - 2)
            pe.wait_ge(S["proj_copied"], 2 * NQKV)
            for t in range(NT):
                ins = pe.transpose(ps[:, 4 + t // 4, (t % 4) * P:(t % 4 + 1) * P], qkv[:, NQKV - 1, t * P:(t + 1) * P], ident[:])
            ins.then_inc(S["v_turned"], 1)

            def scores(u, b, kv, w):
                pe.wait_ge(S["q_staged"], b + 1)
                if not (isinstance(u, int) and u == 0):
                    pe.wait_ge(S["scores_read"], u)
                r = slice(kv * HEAD, (kv + 1) * HEAD)
                for g in range(G):
                    ins = pe.matmul(ps_scores[:, g, 2 * P - w:2 * P], qs[r, g, :], ks[r, 2 * P - w:2 * P], start=True, stop=True)
                ins.then_inc(S["scores_done"], 1)

            def turn_probs(u, buf, w):
                pe.wait_ge(S["probs_ready"], u + 1)
                if not (isinstance(u, int) and u == 0):
                    pe.wait_ge(S["probsT_copied"], u)
                else:
                    pe.wait_ge(S["v_copied"], 1)
                for g in range(G):
                    for cch in range(2 - w // P, 2):
                        ins = pe.transpose(ps_pT[:, g, cch, :], s[:, buf, g, cch * P:(cch + 1) * P], ident[:])
                ins.then_inc(S["probs_turned"], 1)

            def pv(u, b, buf, kv, w):
                pe.wait_ge(S["probsT_copied"], u + 1)
                if not (isinstance(u, int) and u == 0):
                    pe.wait_ge(S["pv_read"], u)
                chunks = range(2 - w // P, 2)
                for g in range(G):
                    for cch in chunks:
                        vals = vtok[:, bass.ds(b - 1 + cch, 1), kv * HEAD:(kv + 1) * HEAD].rearrange("p a d -> p (a d)")
                        ins = pe.matmul(ps_pv[:, g, :], pT[:, buf, g, cch, :], vals, start=cch == chunks[0], stop=cch == 1)
                ins.then_inc(S["pv_done"], 1)

            def turn_attn(b, u):
                pe.wait_ge(S["pv_read"], u + 1)
                pe.wait_ge(S["attn_squared"], b + 1)
                if not (isinstance(b, int) and b == 0):
                    pe.wait_ge(S["attnT_copied"], b)
                for q in range(QC):
                    ins = pe.transpose(ps_turn[:, q, :], attn[:, q * P:(q + 1) * P], ident[:])
                ins.then_inc(S["attn_turned"], 1)

            def sum_conv(i):
                pe.wait_ge(S["conv_squared"], i + 1)
                for t in range(NT):
                    ins = pe.matmul(ps_col[:, bass.ds(i, 1), t:t + 1].rearrange("p a t -> p (a t)"), cbuf[:, 1, t * P:(t + 1) * P], ones[:, 0:1],
                                    start=True, stop=True)
                ins.then_inc(S["conv_summed"], 1)

            def segment(i, g):
                j, half = g // 2, g % 2
                if half == 0:
                    pe.wait_ge(S["wi_lo"], NQKV + 3 * i + j + 1)
                if j == 0 and isinstance(i, int) and i == 0:
                    pe.wait_ge(S["proj_copied"], 2 * NQKV - 1 + half)
                elif j == 0:
                    pe.wait_ge(S["b_used"], 2 * i - 1 + half)
                elif j == 1:
                    pe.wait_ge(S["proj_copied"], 2 * NQKV + 2 * i + half + 1)
                else:
                    pe.wait_ge(S["xc_used"], 2 * i + half + 1)
                project(None, j, half)

            def body(i, first, last):
                u, b = 4 * i, 2 * i
                w0 = P if first else 2 * P
                scores(u, b, 0, w0)
                segment(i, 0)
                scores(u + 1, b, 1, w0)
                if not first:
                    sum_conv(i - 1)
                turn_probs(u, 0, w0)
                segment(i, 1)
                pv(u, b, 0, 0, w0)
                scores(u + 2, b + 1, 0, 2 * P)
                turn_probs(u + 1, 1, w0)
                segment(i, 2)
                pv(u + 1, b, 1, 1, w0)
                scores(u + 3, b + 1, 1, 2 * P)
                turn_probs(u + 2, 0, 2 * P)
                segment(i, 3)
                turn_attn(b, u + 1)
                pv(u + 2, b + 1, 0, 0, 2 * P)
                turn_probs(u + 3, 1, 2 * P)
                segment(i, 4)
                pv(u + 3, b + 1, 1, 1, 2 * P)
                segment(i, 5)
                turn_attn(b + 1, u + 3)

            pe.wait_ge(S["ada2_made"], 4)
            body(0, True, False)
            with pe.Fori(1, CC - 1) as i:
                body(i, False, False)
            body(CC - 1, False, True)
            sum_conv(CC - 1)

            def out_tile(t, par, half, first):
                if half == 0:
                    pe.wait_ge(S["stg_lo"], t + 1)
                if first:
                    if half == 0:
                        pe.wait_ge(S["b_used"], 2 * CC)
                        pe.wait_ge(S["rms_merged"], 1)
                    for n, k in enumerate(CONV_ORDER):
                        pe.wait_ge(S["wo_lo"], n + 1)
                        product(ps[:, 2 * half, :], lambda a_, kk: stg[:, par, a_, kk, :],
                                lambda b_, kk: wo[:, b_, kk, half * HALF:(half + 1) * HALF], [k], n == 0, n == CC - 1)
                    for n, k in enumerate(ATTN_ORDER):
                        pe.wait_ge(S["wo_lo"], CC + n + 1)
                        ins = product(ps[:, 2 * half + 1, :], lambda a_, kk: stg[:, par, a_, kk, :],
                                      lambda b_, kk: wo[:, b_, kk, half * HALF:(half + 1) * HALF], [k], n == 0, n == QC - 1)
                    ins.then_inc(S["out_done"], 1)
                    return
                pe.wait_ge(S["x1_done"], 2 * t - 1 + half)
                for m, order in enumerate((CONV_ORDER, ATTN_ORDER)):
                    ins = product(ps[:, 2 * half + m, :], lambda a_, kk: stg[:, par, a_, kk, :],
                                  lambda b_, kk: wo[:, b_, kk, half * HALF:(half + 1) * HALF], order, True, True)
                ins.then_inc(S["out_done"], 1)

            def turn_h2(t, first):
                pe.wait_ge(S["h2_shifted"], t + 1)
                if first:
                    pe.wait_ge(S["probsT_copied"], 2 * NT)
                else:
                    pe.wait_ge(S["h2_lo"], t)
                for k in range(KC):
                    ins = pe.transpose(ps[:, 4 + k // 4, (k % 4) * P:(k % 4 + 1) * P], htmp[:, k * P:(k + 1) * P], ident[:])
                ins.then_inc(S["h2_turned"], 1)

            out_tile(0, 0, 0, True)
            out_tile(0, 0, 1, True)
            out_tile(1, 1, 0, False)
            out_tile(1, 1, 1, False)
            turn_h2(0, True)
            with pe.Fori(1, NT // 2) as i:
                for par in range(2):
                    out_tile(2 * i + par, par, 0, False)
                    out_tile(2 * i + par, par, 1, False)
                    turn_h2(2 * i + par - 1, False)
            turn_h2(NT - 1, False)

            def gate_up(n, slot, half, first):
                for m, done in enumerate((S["gate_done"], S["up_done"])):
                    if not first:
                        if m == 0:
                            pe.wait_ge(S["silu_done"], 2 * n - 1 + half)
                        else:
                            pe.wait_ge(S["hid_done"], 2 * n - 1 + half)
                    product(ps[:, 2 * half + m, :], lambda a_, k: gu[:, slot, a_, m, k, :],
                            lambda b_, k: h[:, b_, k, half * HALF:(half + 1) * HALF], range(KC), True, True).then_inc(done, 1)

            def down(g, first):
                pe.wait_ge(S["wd_lo"], g + 1)
                for t in range(NT):
                    if t % 4 == 0:
                        pe.wait_ge(S["act_lo"], 4 * g + 3 + t // 4)
                    for half in range(2):
                        m = 2 * t + half
                        if not (first and m < 4):
                            pe.wait_ge(S["res_added"], 2 * NT * g + m - 3)
                        product(ps[:, 4 + m % 4, :], lambda a_, cch: act[:, a_, cch, t * P:(t + 1) * P],
                                lambda b_, cch: wd[:, b_, cch, half * HALF:(half + 1) * HALF], range(2), True, True).then_inc(S["down_done"], 1)

            def ff(g, first):
                for slot in range(2):
                    pe.wait_ge(S["gu_lo"], 2 * g + slot + 1)
                    for half in range(2):
                        gate_up(2 * g + slot, slot, half, first and slot == 0)
                down(g, first)

            pe.wait_ge(S["h2_lo"], NT)
            pe.wait_ge(S["x1_done"], 2 * NT)
            pe.wait_ge(S["x1_squared"], NT)
            ff(0, True)
            with pe.Fori(1, FG) as g:
                ff(g, False)


def bucket_diagonals():
    import math
    import numpy as np
    table = np.zeros((BUCKETS + HQ, DIAGS), np.float32)
    exact = BUCKETS // 2
    for k in range(DIAGS):
        dist = 2 * P - 1 - k
        if 0 <= dist < WINDOW:
            b = dist if dist < exact else min(
                exact + int(math.log(dist / exact) / math.log(MAX_DISTANCE / exact) * (BUCKETS - exact)), BUCKETS - 1)
            table[b, k] = 1.0
        else:
            table[BUCKETS:, k] = MASKED
    return table


_INS = ["x", "c", "rel_bias", "w_ada", "b_ada", "g_norm1", "w_in", "sinks", "conv_w", "g_attn_out",
        "g_conv_out", "w_out", "g_norm2", "w_gu", "w_down", "g_final"]


def kernel(**inputs):
    import numpy as np
    import concourse.bacc as bacc
    from concourse.bass_utils import run_bass_kernel_spmd

    nc = bacc.Bacc("TRN2", target_bir_lowering=False, num_devices=1)
    arrays, args = {}, []
    for name in _INS + ["bucket_table"]:
        a = bucket_diagonals() if name == "bucket_table" else np.ascontiguousarray(inputs[name])
        if name not in ("rel_bias", "g_final", "bucket_table"):
            a = a.reshape(a.shape[1:])
        arrays[f"in_{name}"] = a
        args.append(nc.dram_tensor(f"in_{name}", a.shape, F32, kind="ExternalInput").ap())
    out = nc.dram_tensor("out_0", (SEQ, D), F32, kind="ExternalOutput").ap()
    hymba_layer(nc, *args, out)
    r = run_bass_kernel_spmd(nc, [arrays], core_ids=[0])
    return r.results[0]["out_0"].reshape(1, SEQ, D)
```

```python
from contextlib import ExitStack

import concourse.bass as bass
from concourse import mybir

P = 128
SEQ = 1024
D = 1024
HEAD = 64
HQ = 8
HKV = 2
G = HQ // HKV
ATTN = HQ * HEAD
KVW = HKV * HEAD
CONV = D - ATTN
TAPS = 3
WIDTH_IN = ATTN + 2 * KVW + 3 * CONV
FF = 2816
BUCKETS = 32
WINDOW = 128
MAX_DISTANCE = 128
EPS = 1e-6
MASKED = -1e30

KC = D // P
NT = SEQ // P
HALF = 512
QC = ATTN // P
CC = CONV // P
NQKV = QC + 2
ADA1_BUFS = 3
SLOTS = 3
FG = FF // (2 * P)
DIAGS = 2 * WINDOW + P

V_COND, V_GN1, V_GAIN, V_TAPS = 0, KC, 2 * KC, 3 * KC
V_ROWS = V_TAPS + TAPS * CC

F32 = mybir.dt.float32
F32R = mybir.dt.float32r
I32 = mybir.dt.int32
ALU = mybir.AluOpType
ACT = mybir.ActivationFunctionType
AX = mybir.AxisListType

CONV_ORDER = list(range(QC, KC))
ATTN_ORDER = list(range(QC))
WO_ORDER = CONV_ORDER + ATTN_ORDER
WO_PLACE = [2, 3, 4, 5, 6, 7, 1, 0]
WO_EARLY = 3
WO_AT = {k: WO_PLACE[n] for n, k in enumerate(WO_ORDER)}
WO_BUF = [0, 0, 0, 1, 0, 1, 0, 1]


def hymba_layer(nc, x, c, rel_bias, w_ada, b_ada, g_norm1, w_in, sinks, conv_w, g_attn_out,
                g_conv_out, w_out, g_norm2, w_gu, w_down, g_final, bucket_table, out):
    ctx = ExitStack()
    with ctx:
        def sb(name, shape, dt=F32, stack=ctx):
            return stack.enter_context(nc.sbuf_tensor(name, shape, dt))

        def sem(name):
            return ctx.enter_context(nc.semaphore(name))

        h = sb("h", [P, 2, KC, SEQ], F32R)
        res = sb("res", [P, NT, KC, P])
        rows = sb("rows", [P, 4, D])
        ident = sb("ident", [P, P])
        ones = sb("ones", [P, P])
        vrow = sb("vrow", [V_ROWS, P])
        vcol = sb("vcol", [P, V_ROWS])
        cond = sb("cond", [P, KC])
        mod1 = sb("mod1", [P, 2 * KC])
        sumsq = sb("sumsq", [P, 2 * NT])
        inv = sb("inv", [P, 2 * NT])
        nwt = sb("nwt", [P, 3, 2 * NT])
        addend = sb("addend", [P, 4])
        rtab = sb("rtab", [BUCKETS, HQ])
        sink = sb("sink", [P, HQ])
        nsink = sb("nsink", [P, HQ])
        negmax = sb("negmax", [P, 2, G])
        sinkarg = sb("sinkarg", [P, 2, G])
        psum_p = sb("psum_p", [P, 2, G])
        esink = sb("esink", [P, 2, G])
        den = sb("den", [P, G])
        rden = sb("rden", [P, G])

        with ExitStack() as fa:
            wi_raw = sb("wi_raw", [P, KC, P], F32, fa)
            wi = sb("wi", [P, SLOTS, 2, KC, P], F32R, fa)
            cbuf = sb("cbuf", [P, 2, SEQ], F32, fa)
            qkv = sb("qkv", [P, NQKV, SEQ], F32, fa)
            vtok = sb("vtok", [P, NT, KVW], F32, fa)
            bias = sb("bias", [P, HQ, 2 * P], F32, fa)
            s = sb("s", [P, 2, G, 2 * P], F32, fa)
            pT = sb("pT", [P, 2, G, 2, P], F32, fa)
            attn = sb("attn", [P, ATTN], F32, fa)
            qs = sb("qs", [P, QC, P], F32, fa)
            ks = sb("ks", [P, 2 * P], F32, fa)
        ada1_acc = cbuf[:, :, :].rearrange("p a n -> p (a n)")
        ada1_raw = qkv[:].rearrange("p (a b) n -> p a (b n)", a=ADA1_BUFS)
        ada2_acc = cbuf[:, 0, :]
        btab = attn[0:BUCKETS, 0:DIAGS]
        diag = qs[0:HQ].rearrange("p c q -> p (c q)")[:, 0:DIAGS]

        with ExitStack() as fs:
            sb("skip_s", [P, (KC + SLOTS * 2 * KC) * P + 2 * SEQ + NQKV * SEQ], F32, fs)
            xT = sb("xT", [P, KC, SEQ], F32, fs)

        with ExitStack() as fb:
            wo_raw0 = sb("wo_raw0", [P, D], F32, fb)
            sb("_gu0", [P, 4 * KC * P], F32, fb)
            wo = sb("wo", [P, KC, 2, D], F32R, fb)
            wo_raw1 = sb("wo_raw1", [P, D], F32, fb)
            htmp = sb("htmp", [P, D], F32, fb)
        wo_raw = [wo_raw0, wo_raw1]

        with ExitStack() as fc:
            raw00 = sb("raw00", [P, KC, P], F32, fc)
            gu0 = sb("gu0", [P, 2, 2, KC, P], F32R, fc)
            raw10 = sb("raw10", [P, KC, P], F32, fc)
            raw11 = sb("raw11", [P, KC, P], F32, fc)
            gu1 = sb("gu1", [P, 2, 2, KC, P], F32R, fc)
            wd = sb("wd", [P, 2, 2, D], F32R, fc)
            act = sb("act", [P, 2, 2, SEQ], F32R, fc)
            hid = sb("hid", [P, 2, HALF], F32, fc)
            wd_raw0 = sb("wd_raw0", [P, D], F32, fc)
            raw01 = sb("raw01", [P, KC, P], F32, fc)
            wd_raw1 = sb("wd_raw1", [P, D], F32, fc)
        gu_raw = [[raw00, raw01], [raw10, raw11]]
        gu = [gu0, gu1]
        wd_raw = [wd_raw0, wd_raw1]

        ps = ctx.enter_context(nc.psum_tensor("ps", [P, 8, HALF], F32))
        ps_scores = ps[:, 2:4, :].rearrange("p b (g k) -> p (b g) k", g=2)
        ps_pT = ps[:, 4:6, :].rearrange("p b (g c q) -> p (b g) c q", g=2, c=2)
        ps_pv = ps[:, 6, 0:G * HEAD].rearrange("p (g d) -> p g d", g=G)
        ps_col = ps[:, 6, 256:256 + CC * NT].rearrange("p (i t) -> p i t", i=CC)
        ps_turn = ps[:, 7, :].rearrange("p (c q) -> p c q", c=QC)

        diag_dram = nc.dram_tensor("diag_dram", (HQ, P, DIAGS), F32, kind="Internal").ap()

        names = """vec_loaded bias_row_loaded table_loaded gn2_loaded
            ident_made const_made vec_turned vec_copied cond_made x_summed rms1_made x_scaled x_turned x_copied
            ada1_init ada1_added mod_summed mod_made
            h_full h_hi h_lo_v h_lo_g h_lo_done wi_lo_first
            wi_loaded wi_hi wi_lo proj_done proj_copied xc_used b_used
            ada3_init ada3_init_row ada3_added ada3_summed ada3_made
            ada2_init ada2_init_row ada2_added ada2_summed ada2_made ada2_rows_set
            diag_summed diag_made diag_stored bias_loaded sink_neg
            v_turned v_copied
            q_staged scores_done scores_read max_ready probs_ready probs_turned probsT_copied pv_done pv_read
            attn_squared attn_turned attnT_copied
            conv_base conv_taps conv_squared conv_summed conv_sum_read
            wo_scaled wo_hi wo_lo_early wo_lo rms_merged
            stg_hi stg_lo_first stg_lo out_done x1_done x1_squared h2_scaled h2_shifted h2_turned h2_hi h2_lo
            gu_hi gu_lo wd_scaled wd_hi wd_lo gate_done up_done silu_done hid_done act_hi act_lo
            down_done res_added gf_loaded y_squared y_inv y_scaled y_made_g y_made stored""".split()
        S = {n: sem(n) for n in names}
        x_loaded = [sem(f"x_loaded{t}") for t in range(NT)]
        ada1_loaded = [sem(f"ada1_loaded{b}") for b in range(ADA1_BUFS)]
        ada3_loaded = [sem(f"ada3_loaded{b}") for b in range(2)]
        ada2_loaded = [sem(f"ada2_loaded{b}") for b in range(4)]
        wo_loaded = [sem(f"wo_loaded{b}") for b in range(2)]
        gu_loaded = [sem(f"gu_loaded{b}") for b in range(2)]
        wd_loaded = [sem(f"wd_loaded{b}") for b in range(2)]

        ADA2_RAW = [s[:, 0].rearrange("p g k -> p (g k)"), s[:, 1].rearrange("p g k -> p (g k)"),
                    pT[:, 0].rearrange("p g c q -> p (g c q)"), pT[:, 1].rearrange("p g c q -> p (g c q)")]

        ADA3_RAW = [res[:, :, KC - 1, :], res[:, NT - 2:NT, 0:QC, :].rearrange("p t k n -> p t (k n)")]
        ADA3_ACC = [rows[:, 3, :].rearrange("p (t n) -> p t n", n=P), rows[:, 3, :].rearrange("p (t n) -> p t n", t=2)]

        x_t = x.rearrange("(t p) d -> t p d", p=P)
        out_t = out.rearrange("(t p) d -> t p d", p=P)
        w_in_v = w_in.rearrange("(k p) n -> p k n", p=P)
        w_ada_v = w_ada.rearrange("(k p) n -> k p n", p=P)
        w_out_v = w_out.rearrange("(k p) n -> k p n", p=P)
        w_gu_v = w_gu.rearrange("(k p) (s n) -> p s k n", p=P, s=2)

        def wi_loads(n):
            if n < QC:
                return [(wi_raw[:, :, u * HEAD:(u + 1) * HEAD],
                         w_in_v[:, :, (u * QC + n) * HEAD:(u * QC + n + 1) * HEAD]) for u in range(HKV)]
            return [(wi_raw[:, k:k + KC // 2, :], w_in_v[:, k:k + KC // 2, n * P:(n + 1) * P]) for k in (0, KC // 2)]

        def triple_loads(i, j):
            first = ATTN + 2 * KVW + (CONV, 2 * CONV, 0)[j]
            return [(wi_raw[:, k:k + KC // 2, :],
                     w_in_v[:, k:k + KC // 2, first:first + CONV][:, :, bass.ds(i * P, P)]) for k in (0, KC // 2)]

        LAST_G = [0, 1, 2, 3, 5]
        LAST_V = [4, 6, 7]
        STORE_ORDER = [(t, "y_made_g", n + 1) for n, t in enumerate(LAST_G[:4])]
        STORE_ORDER += [(4, "y_made", 1), (6, "y_made", 2), (5, "y_made_g", 5), (7, "y_made", 3)]

        block = ctx.enter_context(nc.Block())

        @block.sync
        def _(sp):
            for rows_of, first, n in ((c, V_COND, KC), (g_norm1, V_GN1, KC), (g_attn_out, V_GAIN, QC),
                                      (g_conv_out, V_GAIN + QC, CC)):
                sp.dma_start(vrow[first:first + n, :],
                             rows_of.rearrange("(r p) -> r p", p=P)).then_inc(S["vec_loaded"], 16)
            sp.dma_start(vrow[V_TAPS:V_ROWS, :],
                         conv_w.rearrange("j (r p) -> (j r) p", p=P)).then_inc(S["vec_loaded"], 16)
            sp.wait_ge(S["ada1_init"], 1)
            sp.dma_start(ada1_acc[0:1, :], b_ada[0:2 * D].rearrange("(a n) -> a n", a=1)).then_inc(S["bias_row_loaded"], 16)
            for t in range(NT):
                sp.dma_start(res[:, t, :, :].rearrange("p k n -> p (k n)"), x_t[t]).then_inc(x_loaded[t], 16)
            def wait_split(n):
                if isinstance(n, int) and n <= SLOTS:
                    sp.wait_ge(S["wi_lo_first"], n)
                else:
                    sp.wait_ge(S["wi_lo"], n - SLOTS)

            def load_wi(n, loads):
                if not (isinstance(n, int) and n == 0):
                    wait_split(n)
                for dst, src in loads:
                    sp.dma_start(dst, src).then_inc(S["wi_loaded"], 16)

            for k in range(KC):
                if k >= ADA1_BUFS:
                    sp.wait_ge(S["ada1_added"], k - ADA1_BUFS + 1)
                sp.dma_start(ada1_raw[:, k % ADA1_BUFS, :], w_ada_v[k, :, 0:2 * D]).then_inc(ada1_loaded[k % ADA1_BUFS], 16)
                if k in (3, 5, 7):
                    load_wi((k - 3) // 2, wi_loads((k - 3) // 2))
            sp.wait_ge(S["ada2_rows_set"], 1)
            sp.dma_start(rows[:, 2, :], g_norm2.rearrange("(a n) -> a n", a=1).broadcast_to([P, D])).then_inc(S["gn2_loaded"], 16)
            load_wi(SLOTS, wi_loads(SLOTS))
            sp.wait_ge(S["h_lo_done"], 1)
            sp.dma_start(rtab[:], rel_bias).then_inc(S["table_loaded"], 16)
            sp.dma_start(btab, bucket_table[0:BUCKETS, :]).then_inc(S["table_loaded"], 16)
            sp.dma_start(diag, bucket_table[BUCKETS:BUCKETS + HQ, :]).then_inc(S["table_loaded"], 16)
            sp.dma_start(sink[:], sinks.rearrange("(a n) -> a n", a=1).broadcast_to([P, HQ])).then_inc(S["table_loaded"], 16)

            def ada2_loads(v):
                sp.wait_ge(S["ada2_init"], v + 1)
                sp.dma_start(ada2_acc[0:1, :], b_ada.rearrange("(a n) -> a n", a=1)[:, (2 + v) * D:(3 + v) * D]).then_inc(S["ada2_init_row"], 16)
                for k in range(KC):
                    if v == 0 and k < 4:
                        sp.wait_ge(S["h_lo_done"], 1)
                    else:
                        sp.wait_ge(S["ada2_added"], KC * v + k - 3)
                    sp.dma_start(ADA2_RAW[k % 4], w_ada_v[k, :, (2 + v) * D:(3 + v) * D]).then_inc(ada2_loaded[k % 4], 16)

            order = [("a", 0), ("w", 4), ("a", 1), ("w", 5), ("w", 6), ("w", 7), ("w", 8)]
            for kind, n in order:
                if kind == "a":
                    ada2_loads(n)
                elif n < NQKV:
                    load_wi(n, wi_loads(n))
                else:
                    load_wi(n, triple_loads(0, n - NQKV))
                if (kind, n) == ("a", 0):
                    sp.wait_ge(S["diag_made"], 1)
                    sp.dma_start(diag_dram, diag.rearrange("h (a k) -> h a k", a=1).broadcast_to([HQ, P, DIAGS])).then_inc(S["diag_stored"], 16)
                    sp.wait_ge(S["diag_stored"], 16)
                    sp.dma_start(bias[:], bass.AP(tensor=diag_dram.tensor, offset=P - 1,
                                                  ap=[[DIAGS - 1, P], [P * DIAGS, HQ], [1, 2 * P]])).then_inc(S["bias_loaded"], 16)

            for j in range(3):
                load_wi(NQKV + 3 + j, triple_loads(1, j))

            def ada3_load(i, k):
                if k >= 2:
                    sp.wait_ge(S["ada3_added"], KC * (i - 1) + k - 1)
                sp.dma_start(ADA3_RAW[k % 2], w_ada[k * P:(k + 1) * P, bass.ds((i + 3) * D, D)].rearrange(
                    "p (t n) -> p t n", t=NT if k % 2 == 0 else 2)).then_inc(ada3_loaded[k % 2], 16)

            with sp.Fori(1, CC - 1) as i:
                sp.wait_ge(S["ada3_init"], i)
                sp.dma_start(rows[0:1, 3, :], b_ada.rearrange("(a n) -> a n", a=1)[:, bass.ds((i + 3) * D, D)]).then_inc(S["ada3_init_row"], 16)
                ada3_load(i, 0)
                ada3_load(i, 1)
                for j in range(3):
                    load_wi(NQKV + 3 + i * 3 + j, triple_loads(i + 1, j))
                    ada3_load(i, 2 * j + 2)
                    ada3_load(i, 2 * j + 3)

            wait_split(NQKV + 3 * CC)
            for n, k in enumerate(WO_ORDER):
                before = [m for m in range(n) if WO_BUF[m] == WO_BUF[n]]
                if before:
                    m = before[-1]
                    sp.wait_ge(S["wo_hi"], m + 1)
                    if m < WO_EARLY:
                        sp.wait_ge(S["wo_lo_early"], m + 1)
                    else:
                        sp.wait_ge(S["wo_lo"], m + 1 - WO_EARLY)
                elif WO_BUF[n]:
                    sp.wait_ge(S["pv_done"], 2 * NT)
                sp.dma_start(wo_raw[WO_BUF[n]][:], w_out_v[k]).then_inc(wo_loaded[WO_BUF[n]], 16)

            for t in range(NT):
                sp.wait_ge(S["stg_hi"], t + 1)
                if t < 2:
                    sp.wait_ge(S["stg_lo_first"], t + 1)
                else:
                    sp.wait_ge(S["stg_lo"], t - 1)
                sp.dma_start(res[:, t, :, :].rearrange("p k n -> p (k n)"), x_t[t]).then_inc(x_loaded[t], 16)

            sp.wait_ge(S["wo_hi"], KC)
            sp.wait_ge(S["wo_lo"], KC - WO_EARLY)
            sp.dma_start(rows[:, 0, :], g_final.rearrange("(a n) -> a n", a=1).broadcast_to([P, D])).then_inc(S["gf_loaded"], 16)

            def load_gu(g, slot):
                for m in range(2):
                    sp.dma_start(gu_raw[slot][m][:],
                                 w_gu_v[:, m][:, :, bass.ds(g * 2 * P + slot * P, P)]).then_inc(gu_loaded[slot], 16)

            def load_wd(g):
                for cch in range(2):
                    sp.dma_start(wd_raw[cch][:], w_down[bass.ds((2 * g + cch) * P, P), :]).then_inc(wd_loaded[cch], 16)

            load_gu(0, 0)
            sp.wait_ge(S["out_done"], 2 * NT)
            load_gu(0, 1)
            sp.wait_ge(S["h2_turned"], NT)
            load_wd(0)
            with sp.Fori(0, FG - 1) as g:
                for slot in range(2):
                    sp.wait_ge(S["gu_lo"], 2 * g + slot + 1)
                    load_gu(g + 1, slot)
                sp.wait_ge(S["wd_lo"], 2 * g + 2)
                load_wd(g + 1)

            for t, made, count in STORE_ORDER:
                sp.wait_ge(S[made], count)
                sp.dma_start(out_t[t], res[:, t, :, :].rearrange("p k n -> p (k n)")).then_inc(S["stored"], 16)
            sp.wait_ge(S["stored"], 16 * NT)

        @block.gpsimd
        def _(pool):
            pool.memset(ident[:], 0.0)
            pool.memset(ones[:], 1.0).then_inc(S["const_made"], 1)
            pool.drain()
            pool.affine_select(out=ident[:], in_=ident[:], compare_op=ALU.not_equal, fill=1.0, base=0,
                               pattern=[[-1, P]], channel_multiplier=1).then_inc(S["ident_made"], 1)
            for n in range(SLOTS):
                pool.wait_ge(S["wi_hi"], n + 1)
                pool.tensor_tensor(wi[:, n, 1, :, :], wi_raw[:], wi[:, n, 0, :, :], ALU.subtract).then_inc(S["wi_lo_first"], 1)
            for n, k in enumerate(range(2, KC, 3)):
                pool.wait_ge(S["h_hi"], k + 1)
                pool.tensor_tensor(h[:, 1, k, :], xT[:, k, :], h[:, 0, k, :], ALU.subtract).then_inc(S["h_lo_g"], 1)

            def stage_q(b, after):
                if after is not None:
                    pool.wait_ge(S["scores_done"], after)
                w = P if isinstance(b, int) and b == 0 else 2 * P
                pool.tensor_copy(ks[:, 2 * P - w:2 * P], qkv[:, QC, bass.ds((b + 1) * P - w, w)])
                pool.tensor_copy(qs[:], qkv[:, 0:QC, bass.ds(b * P, P)]).then_inc(S["q_staged"], 1)

            pool.wait_ge(S["proj_copied"], 2 * NQKV)
            pool.wait_ge(S["h_lo_done"], 1)
            stage_q(0, None)

            def wo_low_early(n):
                pool.wait_ge(S["wo_hi"], n + 1)
                pool.tensor_tensor(wo[:, WO_PLACE[n], 1, :], wo_raw[0][:], wo[:, WO_PLACE[n], 0, :], ALU.subtract).then_inc(S["wo_lo_early"], 1)

            def body(i, first, last):
                stage_q(2 * i + 1, 4 * i + 2)
                if last:
                    wo_low_early(0)
                pool.wait_ge(S["xc_used"], 2 * i + 2)
                if not first:
                    pool.wait_ge(S["conv_summed"], i)
                pool.tensor_tensor(cbuf[:, 1, :], cbuf[:, 0, :], vcol[:, bass.ds(V_TAPS + 2 * CC + i, 1)].broadcast_to([P, SEQ]),
                                   ALU.mult).then_inc(S["conv_base"], 1)
                if last:
                    wo_low_early(1)
                    wo_low_early(2)
                else:
                    stage_q(2 * i + 2, 4 * i + 4)
                pool.wait_ge(S["b_used"], 2 * i + 2)
                y = res[:, :, bass.ds(QC + i, 1), :].rearrange("p t a n -> p t (a n)")
                pool.tensor_tensor(cbuf[:, 1, :].rearrange("p (t n) -> p t n", t=NT), y, y, ALU.mult).then_inc(S["conv_squared"], 1)

            body(0, True, False)
            with pool.Fori(1, CC - 1) as i:
                body(i, False, False)
            body(CC - 1, False, True)

            def shift(t):
                pool.wait_ge(S["h2_scaled"], t + 1)
                pool.tensor_tensor(htmp[:], htmp[:], rows[:, 1, :], ALU.add).then_inc(S["h2_shifted"], 1)

            for t in range(2, NT):
                pool.wait_ge(S["stg_hi"], t + 1)
                pool.tensor_tensor(h[:, 1, :, t * P:(t + 1) * P], res[:, t, :, :], h[:, 0, :, t * P:(t + 1) * P],
                                   ALU.subtract).then_inc(S["stg_lo"], 1)
                if t >= 4:
                    shift(t - 4)
            for t in range(NT - 4, NT):
                shift(t)

            with pool.Fori(0, FG) as g:
                for cch in range(2):
                    pool.wait_ge(wd_loaded[cch], 16 * g + 16)
                    pool.tensor_tensor(wd_raw[cch][:], wd_raw[cch][:], rows[:, 3, :], ALU.mult).then_inc(S["wd_scaled"], 1)

            pool.wait_ge(S["gf_loaded"], 16)
            for n, t in enumerate(LAST_G):
                pool.wait_ge(S["y_scaled"], n + 1)
                r = res[:, t, :, :].rearrange("p k n -> p (k n)")
                pool.tensor_tensor(r, r, rows[:, 0, :], ALU.mult).then_inc(S["y_made_g"], 1)

        @block.scalar
        def _(a):
            a.wait_ge(S["vec_copied"], 1)
            a.activation(cond[:], vcol[:, V_COND:V_COND + KC], ACT.Silu).then_inc(S["cond_made"], 1)
            for t in range(NT):
                a.wait_ge(x_loaded[t], 16)
                xt = res[:, t, :, :].rearrange("p k n -> p (k n)")
                a.activation(xT[:, 7 if t % 2 else 6, :], xt, ACT.Square, accum_out=sumsq[:, t:t + 1]).then_inc(S["x_summed"], 1)
                a.drain()
            for t in range(NT):
                a.wait_ge(S["x_turned"], t + 1)
                if t == 0:
                    a.drain()
                a.activation(xT[:, :, t * P:(t + 1) * P],
                             ps[:, 2 + 2 * (t % 2):4 + 2 * (t % 2), :].rearrange("p b (k n) -> p (b k) n", n=P),
                             ACT.Copy).then_inc(S["x_copied"], 1)

            def split_wi(n, slot):
                a.wait_ge(S["wi_loaded"], 32 * n + 32)
                if not (isinstance(n, int) and n < SLOTS):
                    a.wait_ge(S["proj_done"], 2 * (n - SLOTS + 1))
                a.activation(wi[:, slot, 0, :, :], wi_raw[:], ACT.Copy).then_inc(S["wi_hi"], 1)

            for n in range(SLOTS):
                split_wi(n, n)
            for k in range(KC):
                a.wait_ge(S["h_full"], k + 1)
                a.activation(h[:, 0, k, :], xT[:, k, :], ACT.Copy).then_inc(S["h_hi"], 1)

            with a.Fori(0, 2) as i:
                for j in range(3):
                    for half in range(2):
                        a.wait_ge(S["proj_done"], (3 * i + j) * 2 + half + 1)
                        a.activation(qkv[:, bass.ds(3 * i + j, 1), half * HALF:(half + 1) * HALF].rearrange("p a n -> p (a n)"),
                                     ps[:, half, :], ACT.Copy).then_inc(S["proj_copied"], 1)
                    split_wi(3 * i + j + SLOTS, j)
            a.wait_ge(S["v_turned"], 1)
            a.activation(vtok[:], ps[:, 4:6, :].rearrange("p b (t n) -> p (b t) n", n=P), ACT.Copy).then_inc(S["v_copied"], 1)
            a.wait_ge(S["max_ready"], 1)

            def exps(u, b, width):
                a.wait_ge(S["max_ready"], u + 1)
                for g in range(G):
                    a.activation(s[:, b, g, 2 * P - width:2 * P], s[:, b, g, 2 * P - width:2 * P], ACT.Exp,
                                 bias=negmax[:, b, g:g + 1], accum_out=psum_p[:, b, g:g + 1])
                a.activation(esink[:, b, :], sinkarg[:, b, :], ACT.Exp).then_inc(S["probs_ready"], 1)

            def copy_pT(u, b, width):
                a.wait_ge(S["probs_turned"], u + 1)
                cs = slice(2 - width // P, 2)
                a.activation(pT[:, b, :, cs, :], ps_pT[:, :, cs, :], ACT.Copy).then_inc(S["probsT_copied"], 1)

            def copy_c(i, half):
                a.wait_ge(S["proj_done"], 2 * (NQKV + 3 * i) + half + 1)
                if half == 0 and not (isinstance(i, int) and i == 0):
                    a.wait_ge(S["conv_taps"], i)
                a.activation(cbuf[:, 0, half * HALF:(half + 1) * HALF], ps[:, 0 + half, :], ACT.Copy).then_inc(S["proj_copied"], 1)

            def copy_attnT(b):
                a.wait_ge(S["attn_turned"], b + 1)
                a.activation(res[:, bass.ds(b, 1), 0:QC, :].rearrange("p a c q -> p (a c) q"), ps_turn, ACT.Copy).then_inc(S["attnT_copied"], 1)

            def square_attn(b, u):
                a.wait_ge(S["pv_read"], u + 1)
                a.activation(junk, attn[:], ACT.Square, accum_out=sumsq[:, bass.ds(b, 1)]).then_inc(S["attn_squared"], 1)
                a.drain()

            junk = ps[:, 7, :]

            def wo_high(n):
                a.wait_ge(S["wo_scaled"], n + 1)
                if n == 0:
                    a.wait_ge(S["q_staged"], NT)
                if n == WO_EARLY:
                    a.wait_ge(S["conv_summed"], CC)
                    a.wait_ge(S["proj_done"], 2 * (NQKV + 3 * CC))
                a.activation(wo[:, WO_PLACE[n], 0, :], wo_raw[WO_BUF[n]][:], ACT.Copy).then_inc(S["wo_hi"], 1)

            def body(i, first, last):
                u, b = 4 * i, 2 * i
                w0 = P if first else 2 * P
                exps(u, 0, w0)
                copy_c(i, 0)
                copy_pT(u, 0, w0)
                exps(u + 1, 1, w0)
                copy_c(i, 1)
                copy_pT(u + 1, 1, w0)
                if not last:
                    split_wi(NQKV + 3 * i + 3, 0)
                exps(u + 2, 0, 2 * P)
                square_attn(b, u + 1)
                copy_pT(u + 2, 0, 2 * P)
                exps(u + 3, 1, 2 * P)
                if last:
                    wo_high(0)
                copy_attnT(b)
                copy_pT(u + 3, 1, 2 * P)
                if last:
                    wo_high(1)
                    wo_high(2)
                else:
                    split_wi(NQKV + 3 * i + 4, 1)
                if not (first or last):
                    a.wait_ge(S["ada3_made"], 2 * i)
                square_attn(b + 1, u + 3)
                copy_attnT(b + 1)
                if not last:
                    split_wi(NQKV + 3 * i + 5, 2)

            body(0, True, False)
            with a.Fori(1, CC - 1) as i:
                body(i, False, False)
            body(CC - 1, False, True)

            def stage_hi(t):
                a.activation(h[:, 0, :, t * P:(t + 1) * P], res[:, t, :, :], ACT.Copy).then_inc(S["stg_hi"], 1)

            a.drain()
            a.wait_ge(S["proj_done"], 2 * (NQKV + 3 * CC))
            a.wait_ge(S["b_used"], 2 * CC)
            stage_hi(0)
            stage_hi(1)
            for n in range(WO_EARLY, KC):
                wo_high(n)
            for t in range(2, 4):
                stage_hi(t)

            def split_gu(g, slot, first=False):
                a.wait_ge(gu_loaded[slot], 32 * g + 32)
                if not first:
                    a.wait_ge(S["up_done"], 4 * (g - 1) + 2 * slot + 2)
                for m in range(2):
                    ins = a.activation(gu[slot][:, 0, m, :, :], gu_raw[slot][m][:], ACT.Copy)
                ins.then_inc(S["gu_hi"], 1)

            def square_x1(t):
                a.wait_ge(S["x1_done"], 2 * t + 2)
                a.activation(ps[:, 6:8, :].rearrange("p b n -> p (b n)"), res[:, bass.ds(t, 1), :, :].rearrange("p a k n -> p (a k n)"), ACT.Square,
                             accum_out=sumsq[:, bass.ds(t, 1)]).then_inc(S["x1_squared"], 1)

            def h2_high(t):
                a.wait_ge(S["h2_turned"], t + 1)
                a.activation(h[:, 0, :, t * P:(t + 1) * P], ps[:, 4:6, :].rearrange("p b (k n) -> p (b k) n", n=P), ACT.Copy).then_inc(S["h2_hi"], 1)

            a.wait_ge(S["x1_done"], 4)
            for t in range(NT):
                if t >= 2:
                    h2_high(t - 2)
                square_x1(t)
                a.drain()
                if t < 4:
                    stage_hi(t + 4)
                if t == 6:
                    split_gu(0, 0, True)
            h2_high(NT - 2)
            h2_high(NT - 1)

            def silu(n, half):
                a.wait_ge(S["gate_done"], 2 * n + half + 1)
                if not (isinstance(n, int) and n == 0):
                    a.wait_ge(S["act_lo"], 2 * n - 1 + half)
                a.activation(hid[:, half, :], ps[:, 2 * half, :], ACT.Silu).then_inc(S["silu_done"], 1)

            def act_high(n, slot, half):
                a.wait_ge(S["hid_done"], 2 * n + half + 1)
                a.activation(act[:, 0, slot, half * HALF:(half + 1) * HALF], hid[:, half, :], ACT.Copy).then_inc(S["act_hi"], 1)

            split_gu(0, 1, True)

            def wd_high(g, first):
                for cch in range(2):
                    a.wait_ge(S["wd_scaled"], 2 * g + cch + 1)
                    if not first:
                        a.wait_ge(S["down_done"], 2 * NT * g)
                    a.activation(wd[:, 0, cch, :], wd_raw[cch][:], ACT.Copy).then_inc(S["wd_hi"], 1)

            def ff(g, first, last):
                if not first:
                    wd_high(g, first)
                for slot in range(2):
                    for half in range(2):
                        silu(2 * g + slot, half)
                        act_high(2 * g + slot, slot, half)
                    if first and slot == 0:
                        wd_high(g, first)
                    if not last:
                        split_gu(g + 1, slot)

            ff(0, True, False)
            with a.Fori(1, FG - 1) as g:
                ff(g, False, False)
            ff(FG - 1, False, True)
            def square_y(t):
                a.wait_ge(S["res_added"], 2 * NT * (FG - 1) + 2 * t + 2)
                if t == 0:
                    a.wait_ge(S["act_lo"], 4 * FG)
                a.activation(hid[:].rearrange("p b n -> p (b n)"), res[:, t, :, :].rearrange("p k n -> p (k n)"), ACT.Square,
                             accum_out=sumsq[:, t:t + 1]).then_inc(S["y_squared"], 1)
                a.drain()

            def scale_y(t):
                a.wait_ge(S["y_inv"], t // 4 + 1)
                r = res[:, t, :, :].rearrange("p k n -> p (k n)")
                a.activation(r, r, ACT.Copy, scale=inv[:, t:t + 1]).then_inc(S["y_scaled"], 1)

            for t in range(4):
                square_y(t)
            for t in range(4):
                scale_y(t)
                square_y(t + 4)
            scale_y(LAST_G[4])

        @block.vector
        def _(v):
            def inv_sqrt(dst, src, width, scale, done=None):
                m, y, w = nwt[:, 0, 0:width], nwt[:, 1, 0:width], nwt[:, 2, 0:width]
                v.tensor_scalar(m, src, scale, EPS, ALU.mult, ALU.add)
                v.drain()
                v.tensor_scalar(w.bitcast(I32), m.bitcast(I32), 1, None, ALU.logical_shift_right)
                v.drain()
                v.tensor_scalar(y.bitcast(I32), w.bitcast(I32), -1, 0x5F3759DF, ALU.mult, ALU.add)
                v.drain()
                for step in range(3):
                    v.tensor_tensor(w, m, y, ALU.mult)
                    v.drain()
                    v.scalar_tensor_tensor(w, w, -0.5, y, ALU.mult, ALU.mult)
                    v.drain()
                    ins = v.scalar_tensor_tensor(dst if step == 2 else y, w, 1.5, y, ALU.add, ALU.mult)
                    if step < 2:
                        v.drain()
                if done is not None:
                    ins.then_inc(done, 1)
                v.drain()

            v.memset(ada1_acc, 0.0).then_inc(S["ada1_init"], 1)
            for r in (0, 1, 3):
                ins = v.memset(rows[:, r, :], 1.0)
            ins.then_inc(S["ada2_rows_set"], 1)
            v.memset(addend[:], 0.0)
            v.drain()
            v.memset(addend[:, 2:3], 1.0)
            v.wait_ge(S["vec_turned"], 1)
            v.tensor_copy(vcol[:], ps[:, 6, 0:V_ROWS]).then_inc(S["vec_copied"], 1)
            for q in range(2):
                v.wait_ge(S["x_summed"], 4 * q + 4)
                inv_sqrt(inv[:, 4 * q:4 * q + 4], sumsq[:, 4 * q:4 * q + 4], 4, 1.0 / D)
                for t in range(4 * q, 4 * q + 4):
                    xt = res[:, t, :, :].rearrange("p k n -> p (k n)")
                    v.tensor_scalar(xt, xt, inv[:, t:t + 1], None, ALU.mult).then_inc(S["x_scaled"], 1)
            v.wait_ge(S["cond_made"], 1)
            v.wait_ge(S["bias_row_loaded"], 16)
            for k in range(KC):
                v.wait_ge(ada1_loaded[k % ADA1_BUFS], 16 * (k // ADA1_BUFS) + 16)
                v.scalar_tensor_tensor(ada1_acc, ada1_raw[:, k % ADA1_BUFS, :], cond[:, k:k + 1], ada1_acc,
                                       ALU.mult, ALU.add).then_inc(S["ada1_added"], 1)
                v.drain()
            def wi_low(n, slot):
                v.wait_ge(S["wi_hi"], n + 1)
                v.tensor_tensor(wi[:, slot, 1, :, :], wi_raw[:], wi[:, slot, 0, :, :], ALU.subtract).then_inc(S["wi_lo"], 1)

            v.wait_ge(S["x_copied"], NT)

            def low(k):
                v.wait_ge(S["h_hi"], k + 1)
                v.tensor_tensor(h[:, 1, k, :], xT[:, k, :], h[:, 0, k, :], ALU.subtract).then_inc(S["h_lo_v"], 1)

            for k in range(KC):
                if k % 2 == 0:
                    v.wait_ge(S["mod_summed"], k // 2 + 1)
                    v.tensor_copy(mod1[:, k:k + 2], ps[:, 7 - k // 2, k:k + 2])
                    v.scalar_tensor_tensor(mod1[:, KC + k:KC + k + 2], ps[:, 7 - k // 2, KC + k:KC + k + 2], 1.0, vcol[:, V_GN1 + k:V_GN1 + k + 2],
                                           ALU.add, ALU.mult).then_inc(S["mod_made"], 1)
                    v.drain()
                v.tensor_scalar(xT[:, k, :], xT[:, k, :], mod1[:, KC + k:KC + k + 1], mod1[:, k:k + 1],
                                ALU.mult, ALU.add).then_inc(S["h_full"], 1)
                if k >= 1 and (k - 1) % 3 != 2:
                    low(k - 1)
            if (KC - 1) % 3 != 2:
                low(KC - 1)
            v.drain()
            v.wait_ge(S["h_lo_g"], len(range(2, KC, 3)))
            v.memset(den[:], 1.0).then_inc(S["h_lo_done"], 1)

            v.wait_ge(S["diag_summed"], 1)
            v.tensor_tensor(diag, ps[0:HQ, 7, 0:DIAGS], diag, ALU.add).then_inc(S["diag_made"], 1)
            v.tensor_scalar(nsink[:], sink[:], -1.0, None, ALU.mult)

            def ada2(r):
                if not (isinstance(r, int) and r == 0):
                    v.wait_ge(S["ada2_summed"], r)
                v.memset(ada2_acc, 0.0).then_inc(S["ada2_init"], 1)
                v.wait_ge(S["ada2_init_row"], 16 * r + 16)
                for k in range(KC):
                    v.drain()
                    v.wait_ge(ada2_loaded[k % 4], 32 * r + 16 * (k // 4) + 16)
                    v.scalar_tensor_tensor(ada2_acc, ADA2_RAW[k % 4], cond[:, k:k + 1], ada2_acc,
                                           ALU.mult, ALU.add).then_inc(S["ada2_added"], 1)

            def ada2_row(r, first):
                v.wait_ge(S["ada2_summed"], r + 1)
                if first:
                    v.wait_ge(S["gn2_loaded"], 16)
                row = rows[:, r, :]
                v.scalar_tensor_tensor(row, ps[:, 6:8, :].rearrange("p b n -> p (b n)"), 0.0, row,
                                       ALU.add, ALU.mult).then_inc(S["ada2_made"], 1)

            ada2(0)
            wi_low(3, 0)
            ada2_row(0, True)
            wi_low(4, 1)
            ada2(1)
            wi_low(5, 2)
            wi_low(6, 0)
            ada2_row(1, False)
            wi_low(7, 1)
            wi_low(8, 2)
            v.drain()
            v.wait_ge(S["bias_loaded"], 16)

            def softmax_head(u, b, width, kv):
                cols = slice(2 * P - width, 2 * P)
                v.wait_ge(S["scores_done"], u + 1)
                if not (isinstance(u, int) and u < 2):
                    v.wait_ge(S["probs_turned"], u - 1)
                v.scalar_tensor_tensor(s[:, b, :, cols], ps_scores[:, :, cols], HEAD ** -0.5,
                                       bias[:, kv * G:(kv + 1) * G, cols], ALU.mult, ALU.add).then_inc(S["scores_read"], 1)
                v.drain()
                v.tensor_reduce(den[:], s[:, b, :, cols], AX.X, ALU.max)
                v.drain()
                v.scalar_tensor_tensor(negmax[:, b, :], den[:], -1.0, nsink[:, kv * G:(kv + 1) * G], ALU.mult, ALU.min)
                v.drain()
                v.tensor_tensor(sinkarg[:, b, :], negmax[:, b, :], sink[:, kv * G:(kv + 1) * G], ALU.add).then_inc(S["max_ready"], 1)

            def normalise(u, b, kv):
                v.wait_ge(S["probs_ready"], u + 1)
                v.tensor_tensor(rden[:], psum_p[:, b, :], esink[:, b, :], ALU.add)
                v.drain()
                v.reciprocal(rden[:], rden[:])
                v.drain()
                v.wait_ge(S["pv_done"], u + 1)
                v.tensor_tensor(attn[:, kv * G * HEAD:(kv + 1) * G * HEAD].rearrange("p (g d) -> p g d", g=G), ps_pv,
                                rden[:].rearrange("p (g a) -> p g a", a=1).broadcast_to([P, G, HEAD]),
                                ALU.mult).then_inc(S["pv_read"], 1)

            def gate_c(i, half):
                v.wait_ge(S["proj_done"], 2 * (NQKV + 3 * i + 1) + half + 1)
                v.wait_ge(S["proj_copied"], 2 * NQKV + 2 * i + half + 1)
                u = cbuf[:, 0, half * HALF:(half + 1) * HALF]
                v.tensor_tensor(u, ps[:, half, :], u, ALU.mult).then_inc(S["xc_used"], 1)

            def taps(i):
                v.wait_ge(S["conv_base"], i + 1)
                for lag in (1, 2):
                    if lag == 2:
                        v.drain()
                    y = cbuf[:, 1, lag:SEQ]
                    ins = v.scalar_tensor_tensor(y, cbuf[:, 0, 0:SEQ - lag], vcol[:, bass.ds(V_TAPS + (2 - lag) * CC + i, 1)], y,
                                                 ALU.mult, ALU.add)
                ins.then_inc(S["conv_taps"], 1)
                v.drain()

            def gate_b(i, half):
                v.wait_ge(S["proj_done"], 2 * (NQKV + 3 * i + 2) + half + 1)
                t0 = half * NT // 2
                v.tensor_tensor(res[:, t0:t0 + NT // 2, bass.ds(QC + i, 1), :].rearrange("p t a n -> p t (a n)"),
                                ps[:, half, :].rearrange("p (t n) -> p t n", n=P),
                                cbuf[:, 1, half * HALF:(half + 1) * HALF].rearrange("p (t n) -> p t n", n=P),
                                ALU.mult).then_inc(S["b_used"], 1)

            def ada3_add(i, k):
                v.drain()
                if k == 0:
                    v.wait_ge(S["ada3_init_row"], 16 * i)
                v.wait_ge(ada3_loaded[k % 2], 64 * (i - 1) + 16 * (k // 2) + 16)
                acc = ADA3_ACC[k % 2]
                v.scalar_tensor_tensor(acc, ADA3_RAW[k % 2], cond[:, k:k + 1], acc, ALU.mult, ALU.add).then_inc(S["ada3_added"], 1)

            def ada3_row(i, half):
                cols = slice(half * HALF, (half + 1) * HALF)
                v.wait_ge(S["ada3_summed"], 2 * (i - 1) + half + 1)
                v.memset(rows[:, 3, cols], 1.0)
                v.drain()
                row = rows[:, bass.ds(i + 1, 1), cols].rearrange("p a n -> p (a n)")
                v.scalar_tensor_tensor(row, ps[:, 7, :], addend[:, bass.ds(i + 1, 1)], row, ALU.add, ALU.mult).then_inc(S["ada3_made"], 1)

            def wo_scale(n):
                k, b = WO_ORDER[n], WO_BUF[n]
                v.wait_ge(wo_loaded[b], 16 * WO_BUF[:n + 1].count(b))
                raw = wo_raw[b][:]
                v.scalar_tensor_tensor(raw, raw, vcol[:, V_GAIN + k:V_GAIN + k + 1], rows[:, 0, :], ALU.mult, ALU.mult).then_inc(S["wo_scaled"], 1)

            def wo_low(n):
                v.wait_ge(S["wo_hi"], n + 1)
                v.tensor_tensor(wo[:, WO_PLACE[n], 1, :], wo_raw[WO_BUF[n]][:], wo[:, WO_PLACE[n], 0, :], ALU.subtract).then_inc(S["wo_lo"], 1)

            def body(i, first, last):
                u = 4 * i
                w0 = P if first else 2 * P
                mid = not (first or last)
                softmax_head(u, 0, w0, 0)
                if mid:
                    v.drain()
                    v.memset(rows[:, 3, :], 0.0).then_inc(S["ada3_init"], 1)
                softmax_head(u + 1, 1, w0, 1)
                if not first:
                    v.wait_ge(S["attn_turned"], 2 * i)
                    v.wait_ge(S["attn_squared"], 2 * i)
                normalise(u, 0, 0)
                softmax_head(u + 2, 0, 2 * P, 0)
                if not last:
                    wi_low(NQKV + 3 * i + 3, 0)
                if mid:
                    ada3_add(i, 0)
                    ada3_add(i, 1)
                if last:
                    wo_scale(0)
                gate_c(i, 0)
                normalise(u + 1, 1, 1)
                softmax_head(u + 3, 1, 2 * P, 1)
                if mid:
                    ada3_add(i, 2)
                    ada3_add(i, 3)
                gate_c(i, 1)
                v.wait_ge(S["attn_turned"], 2 * i + 1)
                v.wait_ge(S["attn_squared"], 2 * i + 1)
                normalise(u + 2, 0, 0)
                if mid:
                    ada3_add(i, 4)
                    ada3_add(i, 5)
                taps(i)
                if last:
                    wo_scale(1)
                else:
                    wi_low(NQKV + 3 * i + 4, 1)
                if mid:
                    ada3_add(i, 6)
                    ada3_add(i, 7)
                    ada3_row(i, 0)
                gate_b(i, 0)
                normalise(u + 3, 1, 1)
                if mid:
                    ada3_row(i, 1)
                if last:
                    wo_scale(2)
                gate_b(i, 1)
                if not last:
                    wi_low(NQKV + 3 * i + 5, 2)

            body(0, True, False)
            with v.Fori(1, CC - 1) as i:
                body(i, False, False)
            body(CC - 1, False, True)

            for t in range(2):
                v.wait_ge(S["stg_hi"], t + 1)
                v.tensor_tensor(h[:, 1, :, t * P:(t + 1) * P], res[:, t, :, :], h[:, 0, :, t * P:(t + 1) * P],
                                ALU.subtract).then_inc(S["stg_lo_first"], 1)
            v.wait_ge(S["conv_summed"], CC)
            v.tensor_reduce(sumsq[:, NT:2 * NT], ps_col.rearrange("p i t -> p t i"), AX.X, ALU.add).then_inc(S["conv_sum_read"], 1)
            wo_scale(WO_EARLY)
            for n in range(WO_EARLY, KC):
                if n + 1 < KC:
                    wo_scale(n + 1)
                wo_low(n)
            v.drain()
            v.wait_ge(S["attn_squared"], NT)
            inv_sqrt(inv[:], sumsq[:], 2 * NT, 1.0 / ATTN, S["rms_merged"])

            def gu_low(g, slot):
                v.wait_ge(S["gu_hi"], 2 * g + slot + 1)
                for m in range(2):
                    ins = v.tensor_tensor(gu[slot][:, 1, m, :, :], gu_raw[slot][m][:], gu[slot][:, 0, m, :, :], ALU.subtract)
                ins.then_inc(S["gu_lo"], 1)

            def norm2(t):
                v.wait_ge(S["x1_squared"], t + 1)
                inv_sqrt(rden[:, 0:1], sumsq[:, t:t + 1], 1, 1.0 / D)
                if t:
                    v.wait_ge(S["h2_turned"], t)
                v.scalar_tensor_tensor(htmp[:], res[:, t, :, :].rearrange("p k n -> p (k n)"), rden[:, 0:1], rows[:, 2, :],
                                       ALU.mult, ALU.mult).then_inc(S["h2_scaled"], 1)

            def h2_low(t):
                v.wait_ge(S["h2_hi"], t + 1)
                v.tensor_tensor(h[:, 1, :, t * P:(t + 1) * P], ps[:, 4:6, :].rearrange("p b (k n) -> p (b k) n", n=P),
                                h[:, 0, :, t * P:(t + 1) * P], ALU.subtract).then_inc(S["h2_lo"], 1)

            def add_out(t):
                v.wait_ge(x_loaded[t], 32)
                for half in range(2):
                    v.wait_ge(S["out_done"], 2 * t + half + 1)
                    bank = 4 * (t == 1) + 2 * half
                    r = res[:, t, half * 4:half * 4 + 4, :].rearrange("p k n -> p (k n)")
                    v.scalar_tensor_tensor(r, ps[:, bank, :], inv[:, NT + t:NT + t + 1], r, ALU.mult, ALU.add)
                    v.drain()
                    v.scalar_tensor_tensor(r, ps[:, bank + 1, :], inv[:, t:t + 1], r, ALU.mult, ALU.add).then_inc(S["x1_done"], 1)

            add_out(0)
            add_out(1)
            norm2(0)
            for t in range(2, NT - 1):
                add_out(t)
                h2_low(t - 2)
                norm2(t - 1)
            h2_low(NT - 3)
            norm2(NT - 2)
            gu_low(0, 0)
            add_out(NT - 1)
            h2_low(NT - 2)
            norm2(NT - 1)
            h2_low(NT - 1)

            def times_up(n, slot, half):
                v.wait_ge(S["silu_done"], 2 * n + half + 1)
                v.wait_ge(S["up_done"], 2 * n + half + 1)
                v.tensor_tensor(hid[:, half, :], ps[:, 2 * half + 1, :], hid[:, half, :], ALU.mult).then_inc(S["hid_done"], 1)
                v.wait_ge(S["act_hi"], 2 * n + half + 1)
                v.tensor_tensor(act[:, 1, slot, half * HALF:(half + 1) * HALF], hid[:, half, :],
                                act[:, 0, slot, half * HALF:(half + 1) * HALF], ALU.subtract).then_inc(S["act_lo"], 1)

            def add_down(g, t, half):
                m = 2 * t + half
                v.wait_ge(S["down_done"], 2 * NT * g + m + 1)
                r = res[:, t, half * 4:half * 4 + 4, :].rearrange("p k n -> p (k n)")
                v.tensor_tensor(r, ps[:, 4 + m % 4, :], r, ALU.add).then_inc(S["res_added"], 1)

            gu_low(0, 1)

            def wd_low(g):
                for cch in range(2):
                    v.wait_ge(S["wd_hi"], 2 * g + cch + 1)
                    v.tensor_tensor(wd[:, 1, cch, :], wd_raw[cch][:], wd[:, 0, cch, :], ALU.subtract).then_inc(S["wd_lo"], 1)

            def ff(g, last, first=False):
                if not first:
                    wd_low(g)
                for slot in range(2):
                    for half in range(2):
                        times_up(2 * g + slot, slot, half)
                    if first and slot == 0:
                        wd_low(g)
                    if slot == 0 and not last:
                        gu_low(g + 1, 0)
                for t in range(NT):
                    for half in range(2):
                        add_down(g, t, half)
                    if t == 2 and not last:
                        gu_low(g + 1, 1)
                    if t == 5 and last:
                        inv_y(0)

            def inv_y(q):
                v.wait_ge(S["y_squared"], 4 * q + 4)
                inv_sqrt(inv[:, 4 * q:4 * q + 4], sumsq[:, 4 * q:4 * q + 4], 4, 1.0 / D, S["y_inv"])

            ff(0, False, True)
            with v.Fori(1, FG - 1) as g:
                ff(g, False)
            ff(FG - 1, True)
            inv_y(1)
            v.wait_ge(S["gf_loaded"], 16)
            for t in LAST_V:
                r = res[:, t, :, :].rearrange("p k n -> p (k n)")
                v.scalar_tensor_tensor(r, r, inv[:, t:t + 1], rows[:, 0, :], ALU.mult, ALU.mult).then_inc(S["y_made"], 1)

        @block.tensor
        def _(pe):
            def product(o, lhs, rhs, ks, first, last):
                ins = None
                for n, k in enumerate(ks):
                    for m, (a_, b_) in enumerate(((0, 0), (0, 1), (1, 0))):
                        ins = pe.matmul(o, lhs(a_, k), rhs(b_, k), start=first and n == 0 and m == 0,
                                        stop=last and n == len(ks) - 1 and m == 2)
                return ins

            pe.wait_ge(S["vec_loaded"], 80)
            pe.wait_ge(S["ident_made"], 1)
            pe.transpose(ps[:, 6, 0:V_ROWS], vrow[:], ident[0:V_ROWS, 0:V_ROWS]).then_inc(S["vec_turned"], 1)
            for t in range(NT):
                pe.wait_ge(S["x_scaled"], t + 1)
                if t >= 2:
                    pe.wait_ge(S["x_copied"], t - 1)
                for k in range(KC):
                    ins = pe.transpose(ps[:, 2 + 2 * (t % 2) + k // 4, (k % 4) * P:(k % 4 + 1) * P], res[:, t, k, :], ident[:])
                ins.then_inc(S["x_turned"], 1)
            pe.wait_ge(S["const_made"], 1)
            pe.wait_ge(S["ada1_added"], KC)
            pe.wait_ge(S["vec_copied"], 1)
            pe.wait_ge(S["x_copied"], NT)
            for k in range(0, KC, 2):
                for n in (k, k + 1, KC + k, KC + k + 1):
                    ins = pe.matmul(ps[:, 7 - k // 2, n:n + 1], ada1_acc[:, n * P:(n + 1) * P], ones[:, 0:1], start=True, stop=True)
                ins.then_inc(S["mod_summed"], 1)

            def project(n, slot, half, order_ready=False):
                o = ps[:, half, :]
                ins = product(o, lambda a_, k: wi[:, slot, a_, k, :],
                              lambda b_, k: h[:, b_, k, half * HALF:(half + 1) * HALF], range(KC), True, True)
                ins.then_inc(S["proj_done"], 1)

            pe.wait_ge(S["wi_lo_first"], 1)
            nv = ng = 0
            for k in range(KC):
                if k % 3 == 2:
                    ng += 1
                    pe.wait_ge(S["h_lo_g"], ng)
                else:
                    nv += 1
                    pe.wait_ge(S["h_lo_v"], nv)
                for half in range(2):
                    ins = product(ps[:, half, :], lambda a_, k: wi[:, 0, a_, k, :],
                                  lambda b_, k: h[:, b_, k, half * HALF:(half + 1) * HALF], [k], k == 0, k == KC - 1)
                    if k == KC - 1:
                        ins.then_inc(S["proj_done"], 1)

            def ada2_sum(r):
                pe.wait_ge(S["ada2_added"], KC * (r + 1))
                if r == 0:
                    pe.wait_ge(S["diag_made"], 1)
                else:
                    pe.wait_ge(S["ada2_made"], r)
                for half in range(2):
                    ins = pe.matmul(ps[:, 6 + half, :], ones[:], ada2_acc[:, half * HALF:(half + 1) * HALF], start=True, stop=True)
                ins.then_inc(S["ada2_summed"], 1)

            pe.wait_ge(S["table_loaded"], 64)
            pe.wait_ge(S["mod_made"], KC // 2)
            pe.matmul(ps[0:HQ, 7, 0:DIAGS], rtab[:], btab, start=True, stop=True).then_inc(S["diag_summed"], 1)
            for n in range(1, NQKV):
                if n < SLOTS:
                    pe.wait_ge(S["wi_lo_first"], n + 1)
                else:
                    pe.wait_ge(S["wi_lo"], n + 1 - SLOTS)
                for half in range(2):
                    pe.wait_ge(S["proj_copied"], 2 * (n - 1) + half + 1)
                    project(n, n % SLOTS, half)
                if n in (2, 4):
                    ada2_sum((n - 2) // 2)
            pe.wait_ge(S["proj_copied"], 2 * NQKV)
            for t in range(NT):
                ins = pe.transpose(ps[:, 4 + t // 4, (t % 4) * P:(t % 4 + 1) * P], qkv[:, NQKV - 1, t * P:(t + 1) * P], ident[:])
            ins.then_inc(S["v_turned"], 1)

            def scores(u, b, kv, w):
                pe.wait_ge(S["q_staged"], b + 1)
                if not (isinstance(u, int) and u == 0):
                    pe.wait_ge(S["scores_read"], u)
                r = slice(kv * HEAD, (kv + 1) * HEAD)
                for g in range(G):
                    ins = pe.matmul(ps_scores[:, g, 2 * P - w:2 * P], qs[r, g, :], ks[r, 2 * P - w:2 * P], start=True, stop=True)
                ins.then_inc(S["scores_done"], 1)

            def turn_probs(u, buf, w):
                pe.wait_ge(S["probs_ready"], u + 1)
                if not (isinstance(u, int) and u == 0):
                    pe.wait_ge(S["probsT_copied"], u)
                else:
                    pe.wait_ge(S["v_copied"], 1)
                for g in range(G):
                    for cch in range(2 - w // P, 2):
                        ins = pe.transpose(ps_pT[:, g, cch, :], s[:, buf, g, cch * P:(cch + 1) * P], ident[:])
                ins.then_inc(S["probs_turned"], 1)

            def pv(u, b, buf, kv, w):
                pe.wait_ge(S["probsT_copied"], u + 1)
                if not (isinstance(u, int) and u == 0):
                    pe.wait_ge(S["pv_read"], u)
                chunks = range(2 - w // P, 2)
                for g in range(G):
                    for cch in chunks:
                        vals = vtok[:, bass.ds(b - 1 + cch, 1), kv * HEAD:(kv + 1) * HEAD].rearrange("p a d -> p (a d)")
                        ins = pe.matmul(ps_pv[:, g, :], pT[:, buf, g, cch, :], vals, start=cch == chunks[0], stop=cch == 1)
                ins.then_inc(S["pv_done"], 1)

            def turn_attn(b, u):
                pe.wait_ge(S["pv_read"], u + 1)
                pe.wait_ge(S["attn_squared"], b + 1)
                if not (isinstance(b, int) and b == 0):
                    pe.wait_ge(S["attnT_copied"], b)
                for q in range(QC):
                    ins = pe.transpose(ps_turn[:, q, :], attn[:, q * P:(q + 1) * P], ident[:])
                ins.then_inc(S["attn_turned"], 1)

            def sum_conv(i):
                pe.wait_ge(S["conv_squared"], i + 1)
                for t in range(NT):
                    ins = pe.matmul(ps_col[:, bass.ds(i, 1), t:t + 1].rearrange("p a t -> p (a t)"), cbuf[:, 1, t * P:(t + 1) * P], ones[:, 0:1],
                                    start=True, stop=True)
                ins.then_inc(S["conv_summed"], 1)

            def segment(i, g):
                j, half = g // 2, g % 2
                if half == 0:
                    pe.wait_ge(S["wi_lo"], NQKV + 3 * i + j + 1 - SLOTS)
                if j == 0 and isinstance(i, int) and i == 0:
                    pe.wait_ge(S["proj_copied"], 2 * NQKV - 1 + half)
                elif j == 0:
                    pe.wait_ge(S["b_used"], 2 * i - 1 + half)
                elif j == 1:
                    pe.wait_ge(S["proj_copied"], 2 * NQKV + 2 * i + half + 1)
                else:
                    pe.wait_ge(S["xc_used"], 2 * i + half + 1)
                project(None, j, half)

            def ada3_sum(i, half):
                pe.wait_ge(S["ada3_added"], KC * i)
                if half == 0:
                    pe.wait_ge(S["attnT_copied"], 2 * i + 1)
                else:
                    pe.wait_ge(S["ada3_made"], 2 * i - 1)
                pe.matmul(ps[:, 7, :], ones[:], rows[:, 3, half * HALF:(half + 1) * HALF], start=True, stop=True).then_inc(S["ada3_summed"], 1)

            def body(i, first, last):
                u, b = 4 * i, 2 * i
                w0 = P if first else 2 * P
                scores(u, b, 0, w0)
                segment(i, 0)
                scores(u + 1, b, 1, w0)
                if not first:
                    sum_conv(i - 1)
                turn_probs(u, 0, w0)
                segment(i, 1)
                pv(u, b, 0, 0, w0)
                scores(u + 2, b + 1, 0, 2 * P)
                turn_probs(u + 1, 1, w0)
                segment(i, 2)
                pv(u + 1, b, 1, 1, w0)
                scores(u + 3, b + 1, 1, 2 * P)
                turn_probs(u + 2, 0, 2 * P)
                segment(i, 3)
                turn_attn(b, u + 1)
                pv(u + 2, b + 1, 0, 0, 2 * P)
                turn_probs(u + 3, 1, 2 * P)
                if not (first or last):
                    ada3_sum(i, 0)
                segment(i, 4)
                if not (first or last):
                    ada3_sum(i, 1)
                pv(u + 3, b + 1, 1, 1, 2 * P)
                segment(i, 5)
                turn_attn(b + 1, u + 3)

            pe.wait_ge(S["ada2_made"], 2)
            body(0, True, False)
            with pe.Fori(1, CC - 1) as i:
                body(i, False, False)
            body(CC - 1, False, True)
            sum_conv(CC - 1)

            def out_part(t, half, k, bank):
                part = WO_ORDER.index(k)
                m = part // QC
                return product(ps[:, bank + 2 * half + m, :], lambda a_, kk: h[:, a_, kk, t * P:(t + 1) * P],
                               lambda b_, kk: wo[:, WO_AT[kk], b_, half * HALF:(half + 1) * HALF], [k],
                               part % QC == 0, part % QC == QC - 1)

            def turn_h2(t):
                pe.wait_ge(S["h2_shifted"], t + 1)
                if t == 0:
                    pe.wait_ge(S["x1_done"], 4)
                else:
                    pe.wait_ge(S["h2_lo"], t)
                for k in range(KC):
                    ins = pe.transpose(ps[:, 4 + k // 4, (k % 4) * P:(k % 4 + 1) * P], htmp[:, k * P:(k + 1) * P], ident[:])
                ins.then_inc(S["h2_turned"], 1)

            pe.wait_ge(S["b_used"], 2 * CC)
            pe.wait_ge(S["attnT_copied"], NT)
            pe.wait_ge(S["stg_lo_first"], 2)
            pe.wait_ge(S["conv_sum_read"], 1)
            for n, k in enumerate(WO_ORDER):
                if n < WO_EARLY:
                    pe.wait_ge(S["wo_lo_early"], n + 1)
                else:
                    pe.wait_ge(S["wo_lo"], n + 1 - WO_EARLY)
                for t in range(2):
                    for half in range(2):
                        ins = out_part(t, half, k, 4 * t)
                        if n == KC - 1:
                            ins.then_inc(S["out_done"], 1)
            for t in range(2, NT):
                pe.wait_ge(S["stg_lo"], t - 1)
                for half in range(2):
                    pe.wait_ge(S["x1_done"], half + 1 if t == 2 else 2 * t - 1 + half)
                    for k in WO_ORDER:
                        ins = out_part(t, half, k, 0)
                    ins.then_inc(S["out_done"], 1)
                    if t == NT - 1 and half == 0:
                        turn_h2(NT - 3)
                if t < NT - 1:
                    turn_h2(t - 2)

            def gate_up(n, slot, half, first):
                for m, done in enumerate((S["gate_done"], S["up_done"])):
                    if not first:
                        if m == 0:
                            pe.wait_ge(S["silu_done"], 2 * n - 1 + half)
                        else:
                            pe.wait_ge(S["hid_done"], 2 * n - 1 + half)
                    product(ps[:, 2 * half + m, :], lambda a_, k: gu[slot][:, a_, m, k, :],
                            lambda b_, k: h[:, b_, k, half * HALF:(half + 1) * HALF], range(KC), True, True).then_inc(done, 1)

            def down(g, first):
                pe.wait_ge(S["wd_lo"], 2 * g + 2)
                for t in range(NT):
                    if t % 4 == 0:
                        pe.wait_ge(S["act_lo"], 4 * g + 3 + t // 4)
                    for half in range(2):
                        m = 2 * t + half
                        if not (first and m < 4):
                            pe.wait_ge(S["res_added"], 2 * NT * g + m - 3)
                        product(ps[:, 4 + m % 4, :], lambda a_, cch: act[:, a_, cch, t * P:(t + 1) * P],
                                lambda b_, cch: wd[:, b_, cch, half * HALF:(half + 1) * HALF], range(2), True, True).then_inc(S["down_done"], 1)

            def ff(g, first):
                for slot in range(2):
                    pe.wait_ge(S["gu_lo"], 2 * g + slot + 1)
                    for half in range(2):
                        gate_up(2 * g + slot, slot, half, first and slot == 0)
                        if first and slot == 0 and half == 0:
                            turn_h2(NT - 1)
                            pe.wait_ge(S["h2_lo"], NT)
                            pe.wait_ge(S["x1_squared"], NT)
                down(g, first)

            pe.wait_ge(S["h2_lo"], NT // 2)
            pe.wait_ge(S["x1_done"], 2 * NT)
            turn_h2(NT - 2)
            ff(0, True)
            with pe.Fori(1, FG) as g:
                ff(g, False)


def bucket_diagonals():
    import math
    import numpy as np
    table = np.zeros((BUCKETS + HQ, DIAGS), np.float32)
    exact = BUCKETS // 2
    for k in range(DIAGS):
        dist = 2 * P - 1 - k
        if 0 <= dist < WINDOW:
            b = dist if dist < exact else min(
                exact + int(math.log(dist / exact) / math.log(MAX_DISTANCE / exact) * (BUCKETS - exact)), BUCKETS - 1)
            table[b, k] = 1.0
        else:
            table[BUCKETS:, k] = MASKED
    return table


_INS = ["x", "c", "rel_bias", "w_ada", "b_ada", "g_norm1", "w_in", "sinks", "conv_w", "g_attn_out",
        "g_conv_out", "w_out", "g_norm2", "w_gu", "w_down", "g_final"]


def kernel(**inputs):
    import numpy as np
    import concourse.bacc as bacc
    from concourse.bass_utils import run_bass_kernel_spmd

    nc = bacc.Bacc("TRN2", target_bir_lowering=False, num_devices=1)
    arrays, args = {}, []
    for name in _INS + ["bucket_table"]:
        a = bucket_diagonals() if name == "bucket_table" else np.ascontiguousarray(inputs[name])
        if name not in ("rel_bias", "g_final", "bucket_table"):
            a = a.reshape(a.shape[1:])
        arrays[f"in_{name}"] = a
        args.append(nc.dram_tensor(f"in_{name}", a.shape, F32, kind="ExternalInput").ap())
    out = nc.dram_tensor("out_0", (SEQ, D), F32, kind="ExternalOutput").ap()
    hymba_layer(nc, *args, out)
    r = run_bass_kernel_spmd(nc, [arrays], core_ids=[0])
    return r.results[0]["out_0"].reshape(1, SEQ, D)
```

```python
from contextlib import ExitStack

import concourse.bass as bass
from concourse import mybir

P = 128
SEQ = 1024
D = 1024
HEAD = 64
HQ = 8
HKV = 2
G = HQ // HKV
ATTN = HQ * HEAD
KVW = HKV * HEAD
CONV = D - ATTN
TAPS = 3
FF = 2816
BUCKETS = 32
WINDOW = 128
MAX_DISTANCE = 128
EPS = 1e-6
MASKED = -1e30

KC = D // P
NT = SEQ // P
HALF = 512
QC = ATTN // P
CC = CONV // P
NQKV = QC + 2
FIRST_LOWS = 2
GROUPS = KC // 2
SLOTS = 3
FG = FF // (2 * P)
DIAGS = 2 * WINDOW + P

V_COND, V_GN1, V_GAIN, V_TAPS = 0, KC, 2 * KC, 3 * KC
V_ROWS = V_TAPS + TAPS * CC

F32 = mybir.dt.float32
F32R = mybir.dt.float32r
I32 = mybir.dt.int32
ALU = mybir.AluOpType
ACT = mybir.ActivationFunctionType
AX = mybir.AxisListType

PIECES = [(k, slice(half * HALF, (half + 1) * HALF)) for half in range(2) for k in range(2)]
PIECES += [(k, slice(0, SEQ)) for k in range(2, KC)]

EARLY_PARTS = [(0, 0), (0, 1), (1, 0)]

CONV_ORDER = list(range(QC, KC))
ATTN_ORDER = list(range(QC))
WO_ORDER = CONV_ORDER + ATTN_ORDER
WO_PLACE = [2, 3, 4, 5, 6, 7, 1, 0]
WO_EARLY = 3
WO_AT = {k: WO_PLACE[n] for n, k in enumerate(WO_ORDER)}
WO_BUF = [0, 0, 0, 1, 0, 2, 1, 0]


def hymba_layer(nc, x, c, rel_bias, w_ada, b_ada, g_norm1, w_in, sinks, conv_w, g_attn_out,
                g_conv_out, w_out, g_norm2, w_gu, w_down, g_final, bucket_table, out):
    ctx = ExitStack()
    with ctx:
        def sb(name, shape, dt=F32, stack=ctx):
            return stack.enter_context(nc.sbuf_tensor(name, shape, dt))

        def sem(name):
            return ctx.enter_context(nc.semaphore(name))

        with ExitStack() as f0:
            ada1_raw = sb("ada1_raw", [P, 2, GROUPS, KC // 2, 2, 2 * P], F32, f0)
        h = sb("h", [P, 2, KC, SEQ], F32R)
        with ExitStack() as f1:
            sb("_tiles", [P, NT // 2 * D], F32, f1)
            qs_low_first = sb("qs_low_first", [P, QC, P], F32R, f1)
            ks_low_first = sb("ks_low_first", [P, P], F32R, f1)
        res = sb("res", [P, NT, KC, P])
        rows = sb("rows", [P, 4, D])
        ident = sb("ident", [P, P])
        ones = sb("ones", [P, P])
        vrow = sb("vrow", [V_ROWS, P])
        vcol = sb("vcol", [P, V_ROWS])
        cond = sb("cond", [P, KC])
        mod1 = sb("mod1", [P, 2 * KC])
        sumsq = sb("sumsq", [P, 2 * NT])
        inv = sb("inv", [P, 2 * NT])
        nwt = sb("nwt", [P, 3, 2 * NT])
        addend = sb("addend", [P, 4])
        rtab = sb("rtab", [BUCKETS, HQ])
        sink = sb("sink", [P, HQ])
        nsink = sb("nsink", [P, HQ])
        negmax = sb("negmax", [P, 2, G])
        sinkarg = sb("sinkarg", [P, 2, G])
        psum_p = sb("psum_p", [P, 2, G])
        esink = sb("esink", [P, 2, G])
        den = sb("den", [P, G])
        rden = sb("rden", [P, G])

        with ExitStack() as fa:
            wi_raw = sb("wi_raw", [P, KC, P], F32, fa)
            wi = sb("wi", [P, SLOTS, 2, KC, P], F32R, fa)
            cbuf = sb("cbuf", [P, 2, SEQ], F32, fa)
            qkv = sb("qkv", [P, NQKV, SEQ], F32, fa)
            vtok = sb("vtok", [P, NT, KVW], F32, fa)
            bias = sb("bias", [P, HQ, 2 * P], F32, fa)
            s = sb("s", [P, 2, G, 2 * P], F32, fa)
            pT = sb("pT", [P, 2, G, 2, P], F32, fa)
            attn = sb("attn", [P, ATTN], F32, fa)
            with ExitStack() as fd:
                diag = sb("diag", [P, DIAGS], F32, fd)[0:HQ]
            qs = sb("qs", [P, QC, P], F32R, fa)
            ks = sb("ks", [P, 2 * P], F32R, fa)
        ada1_acc = cbuf[:, :, :].rearrange("p a n -> p (a n)")
        ada2_acc = cbuf[:, 0, :]
        btab = attn[0:BUCKETS, 0:DIAGS]

        with ExitStack() as fs:
            sb("_before_vtok", [P, (KC + SLOTS * 2 * KC) * P + 2 * SEQ + NQKV * SEQ], F32, fs)
            xT = sb("xT", [P, KC, SEQ], F32, fs)

        with ExitStack() as fl:
            sb("_before_v", [P, (KC + SLOTS * 2 * KC) * P + 2 * SEQ + (NQKV - 1) * SEQ], F32, fl)
            qs_low = sb("qs_low", [P, QC, P], F32R, fl)
            ks_low = sb("ks_low", [P, 2 * P], F32R, fl)

        def lows(b):
            return (qs_low_first, ks_low_first) if isinstance(b, int) and b == 0 else (qs_low, ks_low)

        with ExitStack() as fb:
            wo_raw0 = sb("wo_raw0", [P, D], F32, fb)
            sb("_gu0", [P, 4 * KC * P], F32, fb)
            wo = sb("wo", [P, KC, 2, D], F32R, fb)
            wo_raw1 = sb("wo_raw1", [P, D], F32, fb)
            htmp = sb("htmp", [P, D], F32, fb)
        wo_raw = [wo_raw0, wo_raw1, htmp]

        with ExitStack() as fc:
            raw00 = sb("raw00", [P, KC, P], F32, fc)
            gu0 = sb("gu0", [P, 2, 2, KC, P], F32R, fc)
            raw10 = sb("raw10", [P, KC, P], F32, fc)
            raw11 = sb("raw11", [P, KC, P], F32, fc)
            gu1 = sb("gu1", [P, 2, 2, KC, P], F32R, fc)
            wd = sb("wd", [P, 2, 2, D], F32R, fc)
            act = sb("act", [P, 2, 2, SEQ], F32R, fc)
            hid = sb("hid", [P, 2, HALF], F32, fc)
            wd_raw0 = sb("wd_raw0", [P, D], F32, fc)
            raw01 = sb("raw01", [P, KC, P], F32, fc)
            wd_raw1 = sb("wd_raw1", [P, D], F32, fc)
        gu_raw = [[raw00, raw01], [raw10, raw11]]
        gu = [gu0, gu1]
        wd_raw = [wd_raw0, wd_raw1]

        ps = ctx.enter_context(nc.psum_tensor("ps", [P, 8, HALF], F32))

        def x_banks(t):
            return ps[:, 4 + 2 * (t % 2):6 + 2 * (t % 2), :]

        MOD_BANK = [3, 6, 7, 6]

        ps_scores = ps[:, 2:4, :].rearrange("p b (g k) -> p (b g) k", g=2)
        ps_pT = ps[:, 4:6, :].rearrange("p b (g c q) -> p (b g) c q", g=2, c=2)
        ps_pv = ps[:, 6, 0:G * HEAD].rearrange("p (g d) -> p g d", g=G)
        ps_col = ps[:, 6, 256:256 + CC * NT].rearrange("p (i t) -> p i t", i=CC)
        ps_turn = ps[:, 7, :].rearrange("p (c q) -> p c q", c=QC)

        diag_dram = nc.dram_tensor("diag_dram", (HQ, P, DIAGS), F32, kind="Internal").ap()

        names = """vec_loaded bias_row_loaded table_loaded gn2_loaded
            ident_made const_made vec_turned vec_copied cond_made x_summed x_scaled x_turned x_copied
            ada1_init ada1_added mod_summed mod_made
            h_full h_hi h_lo h_lo_done wi_lo_first
            wi_loaded wi_hi wi_lo proj_done proj_copied xc_used b_used
            ada3_init ada3_init_row ada3_added ada3_summed ada3_made
            ada2_init ada2_init_row ada2_added ada2_summed ada2_made
            diag_summed diag_made diag_stored bias_loaded
            v_turned v_copied
            q_staged scores_done scores_read max_ready probs_ready probs_turned probsT_copied pv_done pv_read
            attn_squared attn_turned attnT_copied
            conv_base conv_taps conv_squared conv_summed conv_sum_read
            wo_scaled wo_hi wo_lo_early wo_lo
            stg_hi stg_lo_first stg_lo out_done x1_done x1_squared h2_scaled h2_shifted h2_turned h2_hi h2_lo
            gu_hi gu_lo wd_scaled wd_hi wd_lo gate_done up_done silu_done hid_done act_hi act_lo
            down_done res_added gf_loaded y_squared y_inv y_gained y_made_v y_made stored""".split()
        S = {n: sem(n) for n in names}
        x_loaded = [sem(f"x_loaded{t}") for t in range(NT)]
        ada1_loaded = [[sem(f"{what}_loaded{g}") for g in range(GROUPS)] for what in ("ada1_first", "ada1_second")]
        ada3_loaded = [sem(f"ada3_loaded{b}") for b in range(2)]
        ada2_loaded = [sem(f"ada2_loaded{b}") for b in range(4)]
        wo_loaded = [sem(f"wo_loaded{b}") for b in range(3)]
        gu_loaded = [sem(f"gu_loaded{b}") for b in range(2)]
        wd_loaded = [sem(f"wd_loaded{b}") for b in range(2)]

        ADA2_RAW = [s[:, 0].rearrange("p g k -> p (g k)"), s[:, 1].rearrange("p g k -> p (g k)"),
                    pT[:, 0].rearrange("p g c q -> p (g c q)"), pT[:, 1].rearrange("p g c q -> p (g c q)")]

        ADA3_RAW = [res[:, :, KC - 1, :], res[:, NT - 2:NT, 0:QC, :].rearrange("p t k n -> p t (k n)")]
        ADA3_ACC = [rows[:, 3, :].rearrange("p (t n) -> p t n", n=P), rows[:, 3, :].rearrange("p (t n) -> p t n", t=2)]

        x_t = x.rearrange("(t p) d -> t p d", p=P)
        out_t = out.rearrange("(t p) d -> t p d", p=P)
        w_in_v = w_in.rearrange("(k p) n -> p k n", p=P)
        w_ada_v = w_ada.rearrange("(k p) n -> k p n", p=P)
        w_out_v = w_out.rearrange("(k p) n -> k p n", p=P)
        w_gu_v = w_gu.rearrange("(k p) (s n) -> p s k n", p=P, s=2)

        def wi_loads(n):
            if n < QC:
                return [(wi_raw[:, :, u * HEAD:(u + 1) * HEAD],
                         w_in_v[:, :, (u * QC + n) * HEAD:(u * QC + n + 1) * HEAD]) for u in range(HKV)]
            return [(wi_raw[:, k:k + KC // 2, :], w_in_v[:, k:k + KC // 2, n * P:(n + 1) * P]) for k in (0, KC // 2)]

        def triple_loads(i, j):
            first = ATTN + 2 * KVW + (CONV, 2 * CONV, 0)[j]
            return [(wi_raw[:, k:k + KC // 2, :],
                     w_in_v[:, k:k + KC // 2, first:first + CONV][:, :, bass.ds(i * P, P)]) for k in (0, KC // 2)]

        block = ctx.enter_context(nc.Block())

        @block.sync
        def _(sp):
            for rows_of, first, n in ((c, V_COND, KC), (g_norm1, V_GN1, KC), (g_attn_out, V_GAIN, QC),
                                      (g_conv_out, V_GAIN + QC, CC)):
                sp.dma_start(vrow[first:first + n, :],
                             rows_of.rearrange("(r p) -> r p", p=P)).then_inc(S["vec_loaded"], 16)
            sp.dma_start(vrow[V_TAPS:V_ROWS, :],
                         conv_w.rearrange("j (r p) -> (j r) p", p=P)).then_inc(S["vec_loaded"], 16)
            sp.wait_ge(S["ada1_init"], 1)
            sp.dma_start(ada1_acc[0:1, :], b_ada[0:2 * D].rearrange("(a n) -> a n", a=1)).then_inc(S["bias_row_loaded"], 16)

            def wait_split(n):
                if isinstance(n, int) and n <= FIRST_LOWS:
                    sp.wait_ge(S["wi_lo_first"], n)
                else:
                    sp.wait_ge(S["wi_lo"], n - FIRST_LOWS)

            def load_wi(n, loads):
                if not (isinstance(n, int) and n == 0):
                    wait_split(n)
                for dst, src in loads:
                    sp.dma_start(dst, src).then_inc(S["wi_loaded"], 16)

            def load_ada1(g):
                for part in range(2):
                    for m in range(2):
                        sp.dma_start(ada1_raw[:, part, g, :, m, :],
                                     w_ada.rearrange("(a k p) n -> a p k n", a=2, p=P)[part][:, :, m * D + g * 2 * P:m * D + (g + 1) * 2 * P]).then_inc(
                            ada1_loaded[part][g], 16)

            load_wi(0, wi_loads(0))
            load_ada1(0)
            for t in range(NT):
                sp.dma_start(res[:, t, :, :].rearrange("p k n -> p (k n)"), x_t[t]).then_inc(x_loaded[t], 16)
            load_wi(1, wi_loads(1))
            load_ada1(1)
            load_wi(2, wi_loads(2))
            load_ada1(2)
            load_ada1(3)
            sp.dma_start(rows[:, 2, :], g_norm2.rearrange("(a n) -> a n", a=1).broadcast_to([P, D])).then_inc(S["gn2_loaded"], 16)
            load_wi(SLOTS, wi_loads(SLOTS))
            sp.wait_ge(S["h_lo_done"], 1)
            sp.dma_start(rtab[:], rel_bias).then_inc(S["table_loaded"], 16)
            sp.dma_start(btab, bucket_table[0:BUCKETS, :]).then_inc(S["table_loaded"], 16)
            sp.dma_start(diag, bucket_table[BUCKETS:BUCKETS + HQ, :]).then_inc(S["table_loaded"], 16)
            sp.dma_start(sink[:], sinks.rearrange("(a n) -> a n", a=1).broadcast_to([P, HQ])).then_inc(S["table_loaded"], 16)

            sp.wait_ge(S["ada2_init"], 1)
            sp.dma_start(ada2_acc[0:1, :], b_ada.rearrange("(a n) -> a n", a=1)[:, 2 * D:3 * D]).then_inc(S["ada2_init_row"], 16)
            for k in range(KC):
                if k >= 4:
                    sp.wait_ge(S["ada2_added"], k - 3)
                sp.dma_start(ADA2_RAW[k % 4], w_ada_v[k, :, 2 * D:3 * D]).then_inc(ada2_loaded[k % 4], 16)
                if k == 3:
                    load_wi(4, wi_loads(4))
            sp.wait_ge(S["diag_made"], 1)
            sp.dma_start(diag_dram, diag.rearrange("h (a k) -> h a k", a=1).broadcast_to([HQ, P, DIAGS])).then_inc(S["diag_stored"], 16)
            load_wi(5, wi_loads(5))
            sp.wait_ge(S["diag_stored"], 16)
            sp.dma_start(bias[:], bass.AP(tensor=diag_dram.tensor, offset=P - 1,
                                          ap=[[DIAGS - 1, P], [P * DIAGS, HQ], [1, 2 * P]])).then_inc(S["bias_loaded"], 16)
            for j in range(3):
                load_wi(NQKV + j, triple_loads(0, j))

            def ada3_load(i, k):
                if k >= 2:
                    sp.wait_ge(S["ada3_added"], KC * i + k - 1)
                sp.dma_start(ADA3_RAW[k % 2], w_ada[k * P:(k + 1) * P, bass.ds((i + 3) * D, D)].rearrange(
                    "p (t n) -> p t n", t=NT if k % 2 == 0 else 2)).then_inc(ada3_loaded[k % 2], 16)

            with sp.Fori(0, CC - 1) as i:
                sp.wait_ge(S["ada3_init"], i + 1)
                sp.dma_start(rows[0:1, 3, :], b_ada.rearrange("(a n) -> a n", a=1)[:, bass.ds((i + 3) * D, D)]).then_inc(S["ada3_init_row"], 16)
                ada3_load(i, 0)
                ada3_load(i, 1)
                load_wi(NQKV + 3 + i * 3, triple_loads(i + 1, 0))
                ada3_load(i, 2)
                ada3_load(i, 3)
                load_wi(NQKV + 3 + i * 3 + 1, triple_loads(i + 1, 1))
                for k in range(4, KC):
                    ada3_load(i, k)
                load_wi(NQKV + 3 + i * 3 + 2, triple_loads(i + 1, 2))

            wait_split(NQKV + 3 * CC)
            for n, k in enumerate(WO_ORDER):
                before = [m for m in range(n) if WO_BUF[m] == WO_BUF[n]]
                if before:
                    m = before[-1]
                    sp.wait_ge(S["wo_hi"], m + 1)
                    if m < WO_EARLY:
                        sp.wait_ge(S["wo_lo_early"], m + 1)
                    else:
                        sp.wait_ge(S["wo_lo"], m + 1 - WO_EARLY)
                elif WO_BUF[n] == 1:
                    sp.wait_ge(S["pv_done"], 2 * NT)
                elif WO_BUF[n] == 2:
                    sp.wait_ge(S["attn_turned"], NT)
                    sp.wait_ge(S["attn_squared"], NT)
                sp.dma_start(wo_raw[WO_BUF[n]][:], w_out_v[k]).then_inc(wo_loaded[WO_BUF[n]], 16)

            for t in range(NT):
                sp.wait_ge(S["stg_hi"], t + 1)
                if t < 2:
                    sp.wait_ge(S["stg_lo_first"], t + 1)
                else:
                    sp.wait_ge(S["stg_lo"], t - 1)
                sp.dma_start(res[:, t, :, :].rearrange("p k n -> p (k n)"), x_t[t]).then_inc(x_loaded[t], 16)

            sp.wait_ge(S["wo_hi"], KC)
            sp.wait_ge(S["wo_lo"], KC - WO_EARLY)
            sp.dma_start(rows[:, 0, :], g_final.rearrange("(a n) -> a n", a=1).broadcast_to([P, D])).then_inc(S["gf_loaded"], 16)

            def load_gu(g, slot):
                for m in range(2):
                    sp.dma_start(gu_raw[slot][m][:],
                                 w_gu_v[:, m][:, :, bass.ds(g * 2 * P + slot * P, P)]).then_inc(gu_loaded[slot], 16)

            def load_wd(g):
                for cch in range(2):
                    sp.dma_start(wd_raw[cch][:], w_down[bass.ds((2 * g + cch) * P, P), :]).then_inc(wd_loaded[cch], 16)

            load_gu(0, 0)
            sp.wait_ge(S["out_done"], 2 * NT)
            load_gu(0, 1)
            sp.wait_ge(S["h2_turned"], NT)
            load_wd(0)
            with sp.Fori(0, FG - 1) as g:
                for slot in range(2):
                    sp.wait_ge(S["gu_lo"], 2 * g + slot + 1)
                    load_gu(g + 1, slot)
                sp.wait_ge(S["wd_lo"], 2 * g + 2)
                load_wd(g + 1)

            for t in range(NT):
                if t < NT - 1:
                    sp.wait_ge(S["y_made"], t + 1)
                else:
                    sp.wait_ge(S["y_made_v"], 1)
                sp.dma_start(out_t[t], res[:, t, :, :].rearrange("p k n -> p (k n)")).then_inc(S["stored"], 16)
            sp.wait_ge(S["stored"], 16 * NT)

        @block.gpsimd
        def _(pool):
            pool.memset(ident[:], 0.0)
            pool.memset(ones[:], 1.0).then_inc(S["const_made"], 1)
            pool.drain()
            pool.affine_select(out=ident[:], in_=ident[:], compare_op=ALU.not_equal, fill=1.0, base=0,
                               pattern=[[-1, P]], channel_multiplier=1).then_inc(S["ident_made"], 1)
            for n in range(FIRST_LOWS):
                pool.wait_ge(S["wi_hi"], n + 1)
                pool.tensor_tensor(wi[:, n, 1, :, :], wi_raw[:], wi[:, n, 0, :, :], ALU.subtract).then_inc(S["wi_lo_first"], 1)
            for n, (k, tokens) in enumerate(PIECES):
                pool.wait_ge(S["h_full"], n + 1)
                pool.tensor_tensor(h[:, 1, k, tokens], xT[:, k, tokens], h[:, 0, k, tokens], ALU.subtract).then_inc(S["h_lo"], 1)

            def stage_q(b, after):
                if after is not None:
                    pool.wait_ge(S["scores_done"], after)
                w = P if isinstance(b, int) and b == 0 else 2 * P
                q, k = qkv[:, 0:QC, bass.ds(b * P, P)], qkv[:, QC, bass.ds((b + 1) * P - w, w)]
                k_part = slice(2 * P - w, 2 * P)
                pool.tensor_copy(ks[:, k_part], k)
                pool.tensor_copy(qs[:], q)
                pool.drain()
                pool.tensor_tensor(lows(b)[1][:], k, ks[:, k_part], ALU.subtract)
                pool.tensor_tensor(lows(b)[0][:], q, qs[:], ALU.subtract).then_inc(S["q_staged"], 1)

            pool.wait_ge(S["proj_copied"], 2 * (NQKV - 1))
            pool.wait_ge(S["h_lo_done"], 1)
            stage_q(0, None)

            def wo_low_early(n):
                pool.wait_ge(S["wo_hi"], n + 1)
                if n == 2:
                    pool.wait_ge(S["scores_done"], 2 * NT)
                pool.tensor_tensor(wo[:, WO_PLACE[n], 1, :], wo_raw[0][:], wo[:, WO_PLACE[n], 0, :], ALU.subtract).then_inc(S["wo_lo_early"], 1)

            def body(i, first, last):
                stage_q(2 * i + 1, 4 * i + 2)
                if last:
                    wo_low_early(0)
                pool.wait_ge(S["xc_used"], 2 * i + 2)
                if not first:
                    pool.wait_ge(S["conv_summed"], i)
                pool.tensor_tensor(cbuf[:, 1, :], cbuf[:, 0, :], vcol[:, bass.ds(V_TAPS + 2 * CC + i, 1)].broadcast_to([P, SEQ]),
                                   ALU.mult).then_inc(S["conv_base"], 1)
                if last:
                    wo_low_early(1)
                else:
                    stage_q(2 * i + 2, 4 * i + 4)
                pool.wait_ge(S["b_used"], 2 * i + 2)
                y = res[:, :, bass.ds(QC + i, 1), :].rearrange("p t a n -> p t (a n)")
                pool.tensor_tensor(cbuf[:, 1, :].rearrange("p (t n) -> p t n", t=NT), y, y, ALU.mult).then_inc(S["conv_squared"], 1)
                if last:
                    wo_low_early(2)

            body(0, True, False)
            with pool.Fori(1, CC - 1) as i:
                body(i, False, False)
            body(CC - 1, False, True)

            def shift(t):
                pool.wait_ge(S["h2_scaled"], t + 1)
                pool.tensor_tensor(htmp[:], htmp[:], rows[:, 1, :], ALU.add).then_inc(S["h2_shifted"], 1)

            for t in range(2, NT):
                pool.wait_ge(S["stg_hi"], t + 1)
                pool.tensor_tensor(h[:, 1, :, t * P:(t + 1) * P], res[:, t, :, :], h[:, 0, :, t * P:(t + 1) * P],
                                   ALU.subtract).then_inc(S["stg_lo"], 1)
            for t in range(NT):
                shift(t)

            with pool.Fori(0, FG) as g:
                for cch in range(2):
                    pool.wait_ge(wd_loaded[cch], 16 * g + 16)
                    pool.tensor_tensor(wd_raw[cch][:], wd_raw[cch][:], rows[:, 3, :], ALU.mult).then_inc(S["wd_scaled"], 1)

            pool.wait_ge(S["gf_loaded"], 16)
            for t in range(NT):
                pool.wait_ge(S["y_squared"], t + 1)
                r = res[:, t, :, :].rearrange("p k n -> p (k n)")
                pool.tensor_tensor(r, r, rows[:, 0, :], ALU.mult).then_inc(S["y_gained"], 1)

        @block.scalar
        def _(a):
            a.wait_ge(S["vec_copied"], 1)
            a.activation(cond[:], vcol[:, V_COND:V_COND + KC], ACT.Silu).then_inc(S["cond_made"], 1)

            def split_wi(n, slot):
                a.wait_ge(S["wi_loaded"], 32 * n + 32)
                if not (isinstance(n, int) and n < SLOTS):
                    a.wait_ge(S["proj_done"], 2 * (n - SLOTS + 1))
                a.activation(wi[:, slot, 0, :, :], wi_raw[:], ACT.Copy).then_inc(S["wi_hi"], 1)

            for t in range(NT):
                if t == 0:
                    split_wi(0, 0)
                a.wait_ge(x_loaded[t], 16)
                xt = res[:, t, :, :].rearrange("p k n -> p (k n)")
                a.activation(xT[:, 7 if t % 2 else 6, :], xt, ACT.Square, accum_out=sumsq[:, t:t + 1]).then_inc(S["x_summed"], 1)
                a.drain()

            def copy_xT(t):
                a.wait_ge(S["x_turned"], t + 1)
                a.activation(xT[:, :, t * P:(t + 1) * P], x_banks(t).rearrange("p b (k n) -> p b k n", n=P), ACT.Copy).then_inc(S["x_copied"], 1)

            def make_h(n):
                k, tokens = PIECES[n]
                a.wait_ge(S["mod_made"], k // 2 + 1)
                a.activation(h[:, 0, k, tokens], xT[:, k, tokens], ACT.Identity, scale=mod1[:, KC + k:KC + k + 1],
                             bias=mod1[:, k:k + 1]).then_inc(S["h_hi"], 1)
                a.activation(xT[:, k, tokens], xT[:, k, tokens], ACT.Identity, scale=mod1[:, KC + k:KC + k + 1],
                             bias=mod1[:, k:k + 1]).then_inc(S["h_full"], 1)

            for t in range(NT // 2):
                copy_xT(t)
            split_wi(1, 1)
            a.drain()
            make_h(0)
            make_h(1)
            for t in range(NT // 2, NT):
                copy_xT(t)
            a.drain()
            for n in range(2, len(PIECES)):
                make_h(n)
                if n == 3:
                    split_wi(2, 2)

            with a.Fori(0, 2) as i:
                for j in range(3):
                    for half in range(2):
                        a.wait_ge(S["proj_done"], (3 * i + j) * 2 + half + 1)
                        a.activation(qkv[:, bass.ds(3 * i + j, 1), half * HALF:(half + 1) * HALF].rearrange("p a n -> p (a n)"),
                                     ps[:, 2 * j + half, :], ACT.Copy).then_inc(S["proj_copied"], 1)
                    split_wi(3 * i + j + SLOTS, j)
            a.wait_ge(S["v_turned"], 1)
            a.activation(vtok[:], ps[:, 4:6, :].rearrange("p b (t n) -> p (b t) n", n=P), ACT.Copy).then_inc(S["v_copied"], 1)
            a.wait_ge(S["max_ready"], 1)

            def exps(u, b, width):
                a.wait_ge(S["max_ready"], u + 1)
                for g in range(G):
                    a.activation(s[:, b, g, 2 * P - width:2 * P], s[:, b, g, 2 * P - width:2 * P], ACT.Exp,
                                 bias=negmax[:, b, g:g + 1], accum_out=psum_p[:, b, g:g + 1])
                a.activation(esink[:, b, :], sinkarg[:, b, :], ACT.Exp).then_inc(S["probs_ready"], 1)

            def copy_pT(u, b, width):
                a.wait_ge(S["probs_turned"], u + 1)
                cs = slice(2 - width // P, 2)
                a.activation(pT[:, b, :, cs, :], ps_pT[:, :, cs, :], ACT.Copy).then_inc(S["probsT_copied"], 1)

            def copy_c(i, half):
                a.wait_ge(S["proj_done"], 2 * (NQKV + 3 * i) + half + 1)
                if half == 0 and not (isinstance(i, int) and i == 0):
                    a.wait_ge(S["conv_taps"], i)
                a.activation(cbuf[:, 0, half * HALF:(half + 1) * HALF], ps[:, 0 + half, :], ACT.Copy).then_inc(S["proj_copied"], 1)

            def copy_attnT(b):
                a.wait_ge(S["attn_turned"], b + 1)
                a.activation(res[:, bass.ds(b, 1), 0:QC, :].rearrange("p a c q -> p (a c) q"), ps_turn, ACT.Copy).then_inc(S["attnT_copied"], 1)

            def square_attn(b, u):
                a.wait_ge(S["pv_read"], u + 1)
                a.activation(junk, attn[:], ACT.Square, accum_out=sumsq[:, bass.ds(b, 1)]).then_inc(S["attn_squared"], 1)
                a.drain()

            junk = ps[:, 7, :]

            def stage_hi(t):
                a.activation(h[:, 0, :, t * P:(t + 1) * P], res[:, t, :, :], ACT.Copy).then_inc(S["stg_hi"], 1)

            def wo_high(n):
                a.wait_ge(S["wo_scaled"], n + 1)
                if n == 0:
                    a.wait_ge(S["q_staged"], NT)
                if n == KC - 2:
                    a.wait_ge(S["conv_summed"], CC)
                    a.wait_ge(S["proj_done"], 2 * (NQKV + 3 * CC))
                a.activation(wo[:, WO_PLACE[n], 0, :], wo_raw[WO_BUF[n]][:], ACT.Copy).then_inc(S["wo_hi"], 1)

            def body(i, first, last):
                u, b = 4 * i, 2 * i
                w0 = P if first else 2 * P
                exps(u, 0, w0)
                copy_c(i, 0)
                copy_pT(u, 0, w0)
                exps(u + 1, 1, w0)
                copy_c(i, 1)
                copy_pT(u + 1, 1, w0)
                if not last:
                    split_wi(NQKV + 3 * i + 3, 0)
                exps(u + 2, 0, 2 * P)
                square_attn(b, u + 1)
                copy_pT(u + 2, 0, 2 * P)
                exps(u + 3, 1, 2 * P)
                if last:
                    wo_high(0)
                copy_attnT(b)
                copy_pT(u + 3, 1, 2 * P)
                if last:
                    wo_high(1)
                    a.wait_ge(S["proj_done"], 2 * (NQKV + 3 * CC) - 1)
                    a.wait_ge(S["b_used"], 2 * CC - 1)
                    stage_hi(0)
                    stage_hi(1)
                    square_attn(b + 1, u + 3)
                    wo_high(2)
                else:
                    split_wi(NQKV + 3 * i + 4, 1)
                    square_attn(b + 1, u + 3)
                if last:
                    wo_high(3)
                copy_attnT(b + 1)
                if not last:
                    split_wi(NQKV + 3 * i + 5, 2)

            body(0, True, False)
            with a.Fori(1, CC - 1) as i:
                body(i, False, False)
            body(CC - 1, False, True)

            a.drain()
            a.wait_ge(S["b_used"], 2 * CC)
            for n in range(WO_EARLY + 1, KC):
                wo_high(n)
            for t in range(2, NT):
                stage_hi(t)

            def split_gu(g, slot, first=False):
                a.wait_ge(gu_loaded[slot], 32 * g + 32)
                if not first:
                    a.wait_ge(S["up_done"], 4 * (g - 1) + 2 * slot + 2)
                for m in range(2):
                    ins = a.activation(gu[slot][:, 0, m, :, :], gu_raw[slot][m][:], ACT.Copy)
                ins.then_inc(S["gu_hi"], 1)

            def square_x1(t):
                a.wait_ge(S["x1_done"], 2 * t + 2)
                a.activation(ps[:, 6:8, :].rearrange("p b n -> p (b n)"), res[:, bass.ds(t, 1), :, :].rearrange("p a k n -> p (a k n)"), ACT.Square,
                             accum_out=sumsq[:, bass.ds(t, 1)]).then_inc(S["x1_squared"], 1)

            def h2_high(t):
                a.wait_ge(S["h2_turned"], t + 1)
                a.activation(h[:, 0, :, t * P:(t + 1) * P], ps[:, 4:6, :].rearrange("p b (k n) -> p (b k) n", n=P), ACT.Copy).then_inc(S["h2_hi"], 1)

            a.wait_ge(S["x1_done"], 4)
            for t in range(NT):
                square_x1(t)
                a.drain()
                if t == 2:
                    h2_high(0)
                if t >= 2:
                    h2_high(t - 1)
                if t == 5:
                    split_gu(0, 0, True)
            h2_high(NT - 1)

            def silu(n, half):
                a.wait_ge(S["gate_done"], 2 * n + half + 1)
                if not (isinstance(n, int) and n == 0):
                    a.wait_ge(S["act_lo"], 2 * n - 1 + half)
                a.activation(hid[:, half, :], ps[:, 2 * half, :], ACT.Silu).then_inc(S["silu_done"], 1)

            def act_high(n, slot, half):
                a.wait_ge(S["hid_done"], 2 * n + half + 1)
                a.activation(act[:, 0, slot, half * HALF:(half + 1) * HALF], hid[:, half, :], ACT.Copy).then_inc(S["act_hi"], 1)

            split_gu(0, 1, True)

            def wd_high(g, first):
                for cch in range(2):
                    a.wait_ge(S["wd_scaled"], 2 * g + cch + 1)
                    if not first:
                        a.wait_ge(S["down_done"], 2 * NT * g)
                    a.activation(wd[:, 0, cch, :], wd_raw[cch][:], ACT.Copy).then_inc(S["wd_hi"], 1)

            def ff(g, first, last):
                if not first:
                    wd_high(g, first)
                for slot in range(2):
                    for half in range(2):
                        silu(2 * g + slot, half)
                        act_high(2 * g + slot, slot, half)
                    if first and slot == 0:
                        wd_high(g, first)
                    if not last:
                        split_gu(g + 1, slot)

            ff(0, True, False)
            with a.Fori(1, FG - 1) as g:
                ff(g, False, False)
            ff(FG - 1, False, True)

            def scale_y(first_tile, end):
                for t in range(first_tile, end):
                    a.wait_ge(S["y_inv"], 1 if t < 4 else 2 if t < 6 else 3)
                    a.wait_ge(S["y_gained"], t + 1)
                    r = res[:, t, :, :].rearrange("p k n -> p (k n)")
                    a.activation(r, r, ACT.Copy, scale=inv[:, t:t + 1]).then_inc(S["y_made"], 1)

            a.wait_ge(S["act_lo"], 4 * FG)
            for t in range(NT):
                a.wait_ge(S["res_added"], 2 * NT * (FG - 1) + 2 * t + 2)
                a.activation(hid[:].rearrange("p b n -> p (b n)"), res[:, t, :, :].rearrange("p k n -> p (k n)"), ACT.Square,
                             accum_out=sumsq[:, t:t + 1]).then_inc(S["y_squared"], 1)
                a.drain()
                if t in (5, 6):
                    scale_y(*((0, 4) if t == 5 else (4, 5)))
            scale_y(5, NT - 1)

        @block.vector
        def _(v):
            def inv_sqrt(dst, src, width, scale, done=None):
                m, y, w = nwt[:, 0, 0:width], nwt[:, 1, 0:width], nwt[:, 2, 0:width]
                v.tensor_scalar(m, src, scale, EPS, ALU.mult, ALU.add)
                v.drain()
                v.tensor_scalar(w.bitcast(I32), m.bitcast(I32), 1, None, ALU.logical_shift_right)
                v.drain()
                v.tensor_scalar(y.bitcast(I32), w.bitcast(I32), -1, 0x5F3759DF, ALU.mult, ALU.add)
                v.drain()
                for step in range(3):
                    v.tensor_tensor(w, m, y, ALU.mult)
                    v.drain()
                    v.scalar_tensor_tensor(w, w, -0.5, y, ALU.mult, ALU.mult)
                    v.drain()
                    ins = v.scalar_tensor_tensor(dst if step == 2 else y, w, 1.5, y, ALU.add, ALU.mult)
                    if step < 2:
                        v.drain()
                if done is not None:
                    ins.then_inc(done, 1)
                v.drain()

            v.memset(ada1_acc, 0.0).then_inc(S["ada1_init"], 1)
            v.memset(rows[:, 1, :], 1.0)
            v.memset(addend[:], 0.0)
            v.drain()
            v.memset(addend[:, 2:3], 1.0)
            v.wait_ge(S["vec_turned"], 1)
            v.tensor_copy(vcol[:], ps[:, 6, 0:V_ROWS]).then_inc(S["vec_copied"], 1)
            v.wait_ge(S["cond_made"], 1)
            v.wait_ge(S["bias_row_loaded"], 16)

            def wi_low(n, slot):
                v.wait_ge(S["wi_hi"], n + 1)
                v.tensor_tensor(wi[:, slot, 1, :, :], wi_raw[:], wi[:, slot, 0, :, :], ALU.subtract).then_inc(S["wi_lo"], 1)

            def ada1_add(g, ks):
                for k in ks:
                    if k % (KC // 2) == 0:
                        v.wait_ge(ada1_loaded[2 * k // KC][g], 32)
                    v.drain()
                    acc = ada1_acc.rearrange("p (m n) -> p m n", m=2)[:, :, g * 2 * P:(g + 1) * 2 * P]
                    ins = v.scalar_tensor_tensor(acc, ada1_raw[:, 2 * k // KC, g, k % (KC // 2), :, :], cond[:, k:k + 1], acc, ALU.mult, ALU.add)
                if k == KC - 1:
                    ins.then_inc(S["ada1_added"], 1)

            def mod(g):
                k = 2 * g
                v.wait_ge(S["mod_summed"], g + 1)
                v.tensor_copy(mod1[:, k:k + 2], ps[:, MOD_BANK[g], k:k + 2])
                v.scalar_tensor_tensor(mod1[:, KC + k:KC + k + 2], ps[:, MOD_BANK[g], KC + k:KC + k + 2], 1.0, vcol[:, V_GN1 + k:V_GN1 + k + 2],
                                       ALU.add, ALU.mult).then_inc(S["mod_made"], 1)

            def x_scale(first_tile, end):
                v.wait_ge(S["x_summed"], end)
                inv_sqrt(inv[:, first_tile:end], sumsq[:, first_tile:end], end - first_tile, 1.0 / D)
                for t in range(first_tile, end):
                    xt = res[:, t, :, :].rearrange("p k n -> p (k n)")
                    v.tensor_scalar(xt, xt, inv[:, t:t + 1], None, ALU.mult).then_inc(S["x_scaled"], 1)

            ada1_add(0, range(KC))
            x_scale(0, NT // 2)
            mod(0)
            x_scale(NT // 2, NT)
            ada1_add(1, range(KC))
            mod(1)
            wi_low(2, 2)
            ada1_add(2, range(KC))
            mod(2)
            ada1_add(3, range(KC))
            mod(3)
            v.drain()
            v.wait_ge(S["h_lo"], len(PIECES))
            v.memset(den[:], 1.0).then_inc(S["h_lo_done"], 1)
            v.wait_ge(S["mod_summed"], GROUPS)
            v.memset(ada2_acc, 0.0).then_inc(S["ada2_init"], 1)

            def ada2_add(k):
                v.drain()
                v.wait_ge(ada2_loaded[k % 4], 16 * (k // 4) + 16)
                v.scalar_tensor_tensor(ada2_acc, ADA2_RAW[k % 4], cond[:, k:k + 1], ada2_acc,
                                       ALU.mult, ALU.add).then_inc(S["ada2_added"], 1)

            wi_low(3, 0)
            v.wait_ge(S["diag_summed"], 1)
            v.tensor_tensor(diag, ps[0:HQ, 7, 0:DIAGS], diag, ALU.add).then_inc(S["diag_made"], 1)
            v.tensor_scalar(nsink[:], sink[:], -1.0, None, ALU.mult)
            v.wait_ge(S["ada2_init_row"], 16)
            for k in range(4):
                ada2_add(k)
            wi_low(4, 1)
            for k in range(4, KC):
                ada2_add(k)
            wi_low(5, 2)
            v.wait_ge(S["ada2_summed"], 1)
            v.tensor_copy(rows[:, 0, :], ps[:, 6:8, :].rearrange("p b n -> p (b n)")).then_inc(S["ada2_made"], 1)
            wi_low(6, 0)
            wi_low(7, 1)
            v.wait_ge(S["gn2_loaded"], 16)
            wi_low(8, 2)
            v.drain()
            v.wait_ge(S["bias_loaded"], 16)

            def softmax_head(u, b, width, kv):
                cols = slice(2 * P - width, 2 * P)
                v.wait_ge(S["scores_done"], u + 1)
                if not (isinstance(u, int) and u < 2):
                    v.wait_ge(S["probs_turned"], u - 1)
                v.scalar_tensor_tensor(s[:, b, :, cols], ps_scores[:, :, cols], HEAD ** -0.5,
                                       bias[:, kv * G:(kv + 1) * G, cols], ALU.mult, ALU.add).then_inc(S["scores_read"], 1)
                v.drain()
                v.tensor_reduce(den[:], s[:, b, :, cols], AX.X, ALU.max)
                v.drain()
                v.scalar_tensor_tensor(negmax[:, b, :], den[:], -1.0, nsink[:, kv * G:(kv + 1) * G], ALU.mult, ALU.min)
                v.drain()
                v.tensor_tensor(sinkarg[:, b, :], negmax[:, b, :], sink[:, kv * G:(kv + 1) * G], ALU.add).then_inc(S["max_ready"], 1)

            def normalise(u, b, kv):
                v.wait_ge(S["probs_ready"], u + 1)
                v.tensor_tensor(rden[:], psum_p[:, b, :], esink[:, b, :], ALU.add)
                v.drain()
                v.reciprocal(rden[:], rden[:])
                v.drain()
                v.wait_ge(S["pv_done"], u + 1)
                v.tensor_tensor(attn[:, kv * G * HEAD:(kv + 1) * G * HEAD].rearrange("p (g d) -> p g d", g=G), ps_pv,
                                rden[:].rearrange("p (g a) -> p g a", a=1).broadcast_to([P, G, HEAD]),
                                ALU.mult).then_inc(S["pv_read"], 1)

            def gate_c(i, half):
                v.wait_ge(S["proj_done"], 2 * (NQKV + 3 * i + 1) + half + 1)
                v.wait_ge(S["proj_copied"], 2 * NQKV + 2 * i + half + 1)
                u = cbuf[:, 0, half * HALF:(half + 1) * HALF]
                v.tensor_tensor(u, ps[:, half, :], u, ALU.mult).then_inc(S["xc_used"], 1)

            def taps(i):
                v.wait_ge(S["conv_base"], i + 1)
                for lag in (1, 2):
                    if lag == 2:
                        v.drain()
                    y = cbuf[:, 1, lag:SEQ]
                    ins = v.scalar_tensor_tensor(y, cbuf[:, 0, 0:SEQ - lag], vcol[:, bass.ds(V_TAPS + (2 - lag) * CC + i, 1)], y,
                                                 ALU.mult, ALU.add)
                ins.then_inc(S["conv_taps"], 1)
                v.drain()

            def gate_b(i, half):
                v.wait_ge(S["proj_done"], 2 * (NQKV + 3 * i + 2) + half + 1)
                t0 = half * NT // 2
                v.tensor_tensor(res[:, t0:t0 + NT // 2, bass.ds(QC + i, 1), :].rearrange("p t a n -> p t (a n)"),
                                ps[:, half, :].rearrange("p (t n) -> p t n", n=P),
                                cbuf[:, 1, half * HALF:(half + 1) * HALF].rearrange("p (t n) -> p t n", n=P),
                                ALU.mult).then_inc(S["b_used"], 1)

            def ada3_add(i, k):
                v.drain()
                if k == 0:
                    v.wait_ge(S["ada3_init_row"], 16 * i + 16)
                v.wait_ge(ada3_loaded[k % 2], 64 * i + 16 * (k // 2) + 16)
                acc = ADA3_ACC[k % 2]
                v.scalar_tensor_tensor(acc, ADA3_RAW[k % 2], cond[:, k:k + 1], acc, ALU.mult, ALU.add).then_inc(S["ada3_added"], 1)

            def ada3_row(i):
                v.wait_ge(S["ada3_summed"], i + 1)
                v.memset(rows[:, 3, :], 1.0)
                v.drain()
                row = rows[:, bass.ds(i + 1, 1), :].rearrange("p a n -> p (a n)")
                v.scalar_tensor_tensor(row, ps[:, 4:6, :].rearrange("p b n -> p (b n)"), addend[:, bass.ds(i + 1, 1)], row,
                                       ALU.add, ALU.mult).then_inc(S["ada3_made"], 1)

            def wo_scale(n):
                k, b = WO_ORDER[n], WO_BUF[n]
                v.wait_ge(wo_loaded[b], 16 * WO_BUF[:n + 1].count(b))
                raw = wo_raw[b][:]
                v.scalar_tensor_tensor(raw, raw, vcol[:, V_GAIN + k:V_GAIN + k + 1], rows[:, 0, :], ALU.mult, ALU.mult).then_inc(S["wo_scaled"], 1)

            def wo_low(n):
                v.wait_ge(S["wo_hi"], n + 1)
                v.tensor_tensor(wo[:, WO_PLACE[n], 1, :], wo_raw[WO_BUF[n]][:], wo[:, WO_PLACE[n], 0, :], ALU.subtract).then_inc(S["wo_lo"], 1)

            def body(i, first, last):
                u = 4 * i
                w0 = P if first else 2 * P
                softmax_head(u, 0, w0, 0)
                if not last:
                    v.drain()
                    v.memset(rows[:, 3, :], 0.0).then_inc(S["ada3_init"], 1)
                softmax_head(u + 1, 1, w0, 1)
                if not last:
                    ada3_add(i, 0)
                    ada3_add(i, 1)
                if not first:
                    v.wait_ge(S["attn_turned"], 2 * i)
                    v.wait_ge(S["attn_squared"], 2 * i)
                normalise(u, 0, 0)
                softmax_head(u + 2, 0, 2 * P, 0)
                if last:
                    wo_scale(0)
                else:
                    wi_low(NQKV + 3 * i + 3, 0)
                    ada3_add(i, 2)
                    ada3_add(i, 3)
                gate_c(i, 0)
                normalise(u + 1, 1, 1)
                softmax_head(u + 3, 1, 2 * P, 1)
                if not last:
                    ada3_add(i, 4)
                    ada3_add(i, 5)
                gate_c(i, 1)
                v.wait_ge(S["attn_turned"], 2 * i + 1)
                v.wait_ge(S["attn_squared"], 2 * i + 1)
                normalise(u + 2, 0, 0)
                taps(i)
                if last:
                    wo_scale(1)
                    gate_b(i, 0)
                    for t in range(2):
                        v.wait_ge(S["stg_hi"], t + 1)
                        v.tensor_tensor(h[:, 1, :, t * P:(t + 1) * P], res[:, t, :, :], h[:, 0, :, t * P:(t + 1) * P],
                                        ALU.subtract).then_inc(S["stg_lo_first"], 1)
                    normalise(u + 3, 1, 1)
                else:
                    ada3_add(i, 6)
                    ada3_add(i, 7)
                    wi_low(NQKV + 3 * i + 4, 1)
                    gate_b(i, 0)
                    normalise(u + 3, 1, 1)
                    ada3_row(i)
                gate_b(i, 1)
                if last:
                    wo_scale(2)
                    wo_scale(3)
                    wo_low(3)
                if not last:
                    wi_low(NQKV + 3 * i + 5, 2)

            body(0, True, False)
            with v.Fori(1, CC - 1) as i:
                body(i, False, False)
            body(CC - 1, False, True)

            v.wait_ge(S["conv_summed"], CC)
            v.tensor_reduce(sumsq[:, NT:2 * NT], ps_col.rearrange("p i t -> p t i"), AX.X, ALU.add).then_inc(S["conv_sum_read"], 1)
            wo_scale(WO_EARLY + 1)
            for n in range(WO_EARLY + 1, KC):
                if n + 1 < KC:
                    wo_scale(n + 1)
                wo_low(n)
            v.drain()
            v.wait_ge(S["attn_squared"], NT)
            inv_sqrt(inv[:], sumsq[:], 2 * NT, 1.0 / ATTN)

            def gu_low(g, slot):
                v.wait_ge(S["gu_hi"], 2 * g + slot + 1)
                for m in range(2):
                    ins = v.tensor_tensor(gu[slot][:, 1, m, :, :], gu_raw[slot][m][:], gu[slot][:, 0, m, :, :], ALU.subtract)
                ins.then_inc(S["gu_lo"], 1)

            def norm2(t):
                v.wait_ge(S["x1_squared"], t + 1)
                inv_sqrt(rden[:, 0:1], sumsq[:, t:t + 1], 1, 1.0 / D)
                if t:
                    v.wait_ge(S["h2_turned"], t)
                v.scalar_tensor_tensor(htmp[:], res[:, t, :, :].rearrange("p k n -> p (k n)"), rden[:, 0:1], rows[:, 2, :],
                                       ALU.mult, ALU.mult).then_inc(S["h2_scaled"], 1)

            def h2_low(t):
                v.wait_ge(S["h2_hi"], t + 1)
                v.tensor_tensor(h[:, 1, :, t * P:(t + 1) * P], ps[:, 4:6, :].rearrange("p b (k n) -> p (b k) n", n=P),
                                h[:, 0, :, t * P:(t + 1) * P], ALU.subtract).then_inc(S["h2_lo"], 1)

            def add_out(t):
                v.wait_ge(x_loaded[t], 32)
                for half in range(2):
                    v.wait_ge(S["out_done"], 2 * t + half + 1)
                    bank = 4 * (t == 1) + 2 * half
                    r = res[:, t, half * 4:half * 4 + 4, :].rearrange("p k n -> p (k n)")
                    v.scalar_tensor_tensor(r, ps[:, bank, :], inv[:, NT + t:NT + t + 1], r, ALU.mult, ALU.add)
                    v.drain()
                    v.scalar_tensor_tensor(r, ps[:, bank + 1, :], inv[:, t:t + 1], r, ALU.mult, ALU.add).then_inc(S["x1_done"], 1)

            add_out(0)
            add_out(1)
            norm2(0)
            add_out(2)
            norm2(1)
            h2_low(0)
            norm2(2)
            h2_low(1)
            for t in range(3, NT - 1):
                add_out(t)
                h2_low(t - 1)
                norm2(t)
                if t == 5:
                    gu_low(0, 0)
            add_out(NT - 1)
            norm2(NT - 1)
            h2_low(NT - 2)
            h2_low(NT - 1)

            def times_up(n, slot, half):
                v.wait_ge(S["silu_done"], 2 * n + half + 1)
                v.wait_ge(S["up_done"], 2 * n + half + 1)
                v.tensor_tensor(hid[:, half, :], ps[:, 2 * half + 1, :], hid[:, half, :], ALU.mult).then_inc(S["hid_done"], 1)
                v.wait_ge(S["act_hi"], 2 * n + half + 1)
                v.tensor_tensor(act[:, 1, slot, half * HALF:(half + 1) * HALF], hid[:, half, :],
                                act[:, 0, slot, half * HALF:(half + 1) * HALF], ALU.subtract).then_inc(S["act_lo"], 1)

            def add_down(g, t, half):
                m = 2 * t + half
                v.wait_ge(S["down_done"], 2 * NT * g + m + 1)
                r = res[:, t, half * 4:half * 4 + 4, :].rearrange("p k n -> p (k n)")
                v.tensor_tensor(r, ps[:, 4 + m % 4, :], r, ALU.add).then_inc(S["res_added"], 1)

            gu_low(0, 1)

            def wd_low(g):
                for cch in range(2):
                    v.wait_ge(S["wd_hi"], 2 * g + cch + 1)
                    v.tensor_tensor(wd[:, 1, cch, :], wd_raw[cch][:], wd[:, 0, cch, :], ALU.subtract).then_inc(S["wd_lo"], 1)

            def ff(g, last, first=False):
                if not first:
                    wd_low(g)
                for slot in range(2):
                    for half in range(2):
                        times_up(2 * g + slot, slot, half)
                    if first and slot == 0:
                        wd_low(g)
                    if slot == 0 and not last:
                        gu_low(g + 1, 0)
                for t in range(NT):
                    for half in range(2):
                        add_down(g, t, half)
                    if t == 2 and not last:
                        gu_low(g + 1, 1)
                    if last and t in (4, 6):
                        inv_y(0 if t == 4 else 4, t)
                if last:
                    inv_y(6, NT)
                    t = NT - 1
                    v.wait_ge(S["y_gained"], NT)
                    r = res[:, t, :, :].rearrange("p k n -> p (k n)")
                    v.tensor_scalar(r, r, inv[:, t:t + 1], None, ALU.mult).then_inc(S["y_made_v"], 1)

            def inv_y(first_tile, end):
                v.wait_ge(S["y_squared"], end)
                inv_sqrt(inv[:, first_tile:end], sumsq[:, first_tile:end], end - first_tile, 1.0 / D, S["y_inv"])

            ff(0, False, True)
            with v.Fori(1, FG - 1) as g:
                ff(g, False)
            ff(FG - 1, True)

        @block.tensor
        def _(pe):
            def product(o, lhs, rhs, ks, first, last):
                ins = None
                for n, k in enumerate(ks):
                    for m, (a_, b_) in enumerate(((0, 0), (0, 1), (1, 0))):
                        ins = pe.matmul(o, lhs(a_, k), rhs(b_, k), start=first and n == 0 and m == 0,
                                        stop=last and n == len(ks) - 1 and m == 2)
                return ins

            pe.wait_ge(S["vec_loaded"], 80)
            pe.wait_ge(S["ident_made"], 1)
            pe.transpose(ps[:, 6, 0:V_ROWS], vrow[:], ident[0:V_ROWS, 0:V_ROWS]).then_inc(S["vec_turned"], 1)
            def mod_sum(g):
                if g >= 2:
                    pe.wait_ge(S["mod_made"], g - 1)
                pe.wait_ge(S["ada1_added"], g + 1)
                for n in (2 * g, 2 * g + 1, KC + 2 * g, KC + 2 * g + 1):
                    ins = pe.matmul(ps[:, MOD_BANK[g], n:n + 1], ada1_acc[:, n * P:(n + 1) * P], ones[:, 0:1], start=True, stop=True)
                ins.then_inc(S["mod_summed"], 1)

            def project(bank, slot, half):
                ins = product(ps[:, bank, :], lambda a_, k: wi[:, slot, a_, k, :],
                              lambda b_, k: h[:, b_, k, half * HALF:(half + 1) * HALF], range(KC), True, True)
                ins.then_inc(S["proj_done"], 1)

            def project_group(n, g, b_, halves=(0, 1)):
                for k in (2 * g, 2 * g + 1):
                    if n == 0:
                        pe.wait_ge(S["h_lo" if b_ else "h_hi"], k + 1 + 2 * (1 if g else halves[-1]))
                    for half in halves:
                        for a_ in ((0,) if b_ else (0, 1)):
                            ins = pe.matmul(ps[:, 2 * n + half, :], wi[:, n, a_, k, :], h[:, b_, k, half * HALF:(half + 1) * HALF],
                                            start=k == 0 and b_ == 0 and a_ == 0, stop=k == KC - 1 and b_ == 1)
                        if k == KC - 1 and b_ == 1:
                            ins.then_inc(S["proj_done"], 1)

            def turn_x(t):
                pe.wait_ge(S["x_scaled"], t + 1)
                if t >= 2:
                    pe.wait_ge(S["x_copied"], t - 1)
                for k in range(KC):
                    ins = pe.transpose(x_banks(t)[:, k // 4, (k % 4) * P:(k % 4 + 1) * P], res[:, t, k, :], ident[:])
                ins.then_inc(S["x_turned"], 1)

            turn_x(0)
            turn_x(1)
            pe.wait_ge(S["const_made"], 1)
            pe.wait_ge(S["vec_copied"], 1)
            mod_sum(0)
            for t in range(2, 6):
                turn_x(t)
            pe.wait_ge(S["wi_lo_first"], 1)
            project_group(0, 0, 0, (0,))
            pe.wait_ge(S["wi_lo_first"], 2)
            project_group(1, 0, 0, (0,))
            turn_x(6)
            turn_x(7)
            project_group(0, 0, 1, (0,))
            project_group(1, 0, 1, (0,))
            pe.wait_ge(S["x_copied"], NT)
            mod_sum(1)
            for b_ in range(2):
                for n in range(2):
                    project_group(n, 0, b_, (1,))
            pe.wait_ge(S["wi_lo"], 1)
            project_group(2, 0, 0)
            project_group(2, 0, 1)
            for g in range(1, GROUPS):
                for n in range(SLOTS):
                    if n == SLOTS - 1 and g < GROUPS - 1:
                        mod_sum(g + 1)
                    project_group(n, g, 0)
                for n in range(SLOTS):
                    project_group(n, g, 1)

            pe.wait_ge(S["table_loaded"], 64)
            pe.wait_ge(S["mod_made"], GROUPS)
            pe.matmul(ps[0:HQ, 7, 0:DIAGS], rtab[:], btab, start=True, stop=True).then_inc(S["diag_summed"], 1)
            for n in range(SLOTS, NQKV):
                pe.wait_ge(S["wi_lo"], n + 1 - FIRST_LOWS)
                for half in range(2):
                    pe.wait_ge(S["proj_copied"], 2 * (n - SLOTS) + half + 1)
                    project(2 * (n - SLOTS) + half, n % SLOTS, half)
                if n == NQKV - 2:
                    pe.wait_ge(S["ada2_added"], KC)
                    pe.wait_ge(S["diag_made"], 1)
                    for half in range(2):
                        ins = pe.matmul(ps[:, 6 + half, :], ones[:], ada2_acc[:, half * HALF:(half + 1) * HALF], start=True, stop=True)
                    ins.then_inc(S["ada2_summed"], 1)
            def scores(u, b, kv, w):
                pe.wait_ge(S["q_staged"], b + 1)
                if not (isinstance(u, int) and u == 0):
                    pe.wait_ge(S["scores_read"], u)
                r = slice(kv * HEAD, (kv + 1) * HEAD)
                for g in range(G):
                    k_high = ks[:, 2 * P - w:2 * P]
                    for m, (q, k) in enumerate(((qs, k_high), (qs, lows(b)[1]), (lows(b)[0], k_high))):
                        ins = pe.matmul(ps_scores[:, g, 2 * P - w:2 * P], q[r, g, :], k[r, :], start=m == 0, stop=m == 2)
                ins.then_inc(S["scores_done"], 1)

            def turn_probs(u, buf, w):
                pe.wait_ge(S["probs_ready"], u + 1)
                if not (isinstance(u, int) and u == 0):
                    pe.wait_ge(S["probsT_copied"], u)
                else:
                    pe.wait_ge(S["v_copied"], 1)
                for g in range(G):
                    for cch in range(2 - w // P, 2):
                        ins = pe.transpose(ps_pT[:, g, cch, :], s[:, buf, g, cch * P:(cch + 1) * P], ident[:])
                ins.then_inc(S["probs_turned"], 1)

            def pv(u, b, buf, kv, w):
                pe.wait_ge(S["probsT_copied"], u + 1)
                if not (isinstance(u, int) and u == 0):
                    pe.wait_ge(S["pv_read"], u)
                chunks = range(2 - w // P, 2)
                for g in range(G):
                    for cch in chunks:
                        vals = vtok[:, bass.ds(b - 1 + cch, 1), kv * HEAD:(kv + 1) * HEAD].rearrange("p a d -> p (a d)")
                        ins = pe.matmul(ps_pv[:, g, :], pT[:, buf, g, cch, :], vals, start=cch == chunks[0], stop=cch == 1)
                ins.then_inc(S["pv_done"], 1)

            def turn_attn(b, u):
                pe.wait_ge(S["pv_read"], u + 1)
                pe.wait_ge(S["attn_squared"], b + 1)
                if not (isinstance(b, int) and b == 0):
                    pe.wait_ge(S["attnT_copied"], b)
                for q in range(QC):
                    ins = pe.transpose(ps_turn[:, q, :], attn[:, q * P:(q + 1) * P], ident[:])
                ins.then_inc(S["attn_turned"], 1)

            def sum_conv(i):
                pe.wait_ge(S["conv_squared"], i + 1)
                for t in range(NT):
                    ins = pe.matmul(ps_col[:, bass.ds(i, 1), t:t + 1].rearrange("p a t -> p (a t)"), cbuf[:, 1, t * P:(t + 1) * P], ones[:, 0:1],
                                    start=True, stop=True)
                ins.then_inc(S["conv_summed"], 1)

            def segment(i, g):
                j, half = g // 2, g % 2
                if half == 0:
                    pe.wait_ge(S["wi_lo"], NQKV + 3 * i + j + 1 - FIRST_LOWS)
                if j == 0 and isinstance(i, int) and i == 0:
                    pe.wait_ge(S["proj_copied"], 2 * NQKV - 1 + half)
                elif j == 0:
                    pe.wait_ge(S["b_used"], 2 * i - 1 + half)
                elif j == 1:
                    pe.wait_ge(S["proj_copied"], 2 * NQKV + 2 * i + half + 1)
                else:
                    pe.wait_ge(S["xc_used"], 2 * i + half + 1)
                project(half, j, half)

            def out_part(t, half, k, bank):
                part = WO_ORDER.index(k)
                m = part // QC
                return product(ps[:, bank + 2 * half + m, :], lambda a_, kk: h[:, a_, kk, t * P:(t + 1) * P],
                               lambda b_, kk: wo[:, WO_AT[kk], b_, half * HALF:(half + 1) * HALF], [k],
                               part % QC == 0, part % QC == QC - 1)

            def ada3_sum(i):
                pe.wait_ge(S["ada3_added"], KC * (i + 1))
                pe.wait_ge(S["probsT_copied"], 4 * i + 4)
                for half in range(2):
                    ins = pe.matmul(ps[:, 4 + half, :], ones[:], rows[:, 3, half * HALF:(half + 1) * HALF], start=True, stop=True)
                ins.then_inc(S["ada3_summed"], 1)

            def body(i, first, last):
                u, b = 4 * i, 2 * i
                w0 = P if first else 2 * P
                scores(u, b, 0, w0)
                if first:
                    pe.wait_ge(S["proj_copied"], 2 * NQKV)
                    for t in range(NT):
                        ins = pe.transpose(ps[:, 4 + t // 4, (t % 4) * P:(t % 4 + 1) * P], qkv[:, NQKV - 1, t * P:(t + 1) * P], ident[:])
                    ins.then_inc(S["v_turned"], 1)
                segment(i, 0)
                scores(u + 1, b, 1, w0)
                if not first:
                    sum_conv(i - 1)
                turn_probs(u, 0, w0)
                segment(i, 1)
                pv(u, b, 0, 0, w0)
                scores(u + 2, b + 1, 0, 2 * P)
                turn_probs(u + 1, 1, w0)
                segment(i, 2)
                pv(u + 1, b, 1, 1, w0)
                scores(u + 3, b + 1, 1, 2 * P)
                turn_probs(u + 2, 0, 2 * P)
                segment(i, 3)
                turn_attn(b, u + 1)
                pv(u + 2, b + 1, 0, 0, 2 * P)
                turn_probs(u + 3, 1, 2 * P)
                segment(i, 4)
                pv(u + 3, b + 1, 1, 1, 2 * P)
                if not last:
                    ada3_sum(i)
                segment(i, 5)
                if last:
                    pe.wait_ge(S["stg_lo_first"], 2)
                    pe.wait_ge(S["b_used"], 2 * CC - 1)
                    for n in range(2):
                        pe.wait_ge(S["wo_lo_early"], n + 1)
                        for t, half in EARLY_PARTS:
                            out_part(t, half, WO_ORDER[n], 4 * t)
                    turn_attn(b + 1, u + 3)
                else:
                    turn_attn(b + 1, u + 3)
                    pe.wait_ge(S["ada3_made"], i + 1)

            pe.wait_ge(S["ada2_made"], 1)
            body(0, True, False)
            with pe.Fori(1, CC - 1) as i:
                body(i, False, False)
            body(CC - 1, False, True)
            sum_conv(CC - 1)

            def turn_h2(t):
                pe.wait_ge(S["h2_shifted"], t + 1)
                if t == 0:
                    pe.wait_ge(S["x1_done"], 4)
                else:
                    pe.wait_ge(S["h2_lo"], t)
                for k in range(KC):
                    ins = pe.transpose(ps[:, 4 + k // 4, (k % 4) * P:(k % 4 + 1) * P], htmp[:, k * P:(k + 1) * P], ident[:])
                ins.then_inc(S["h2_turned"], 1)

            pe.wait_ge(S["b_used"], 2 * CC)
            pe.wait_ge(S["attnT_copied"], NT)
            pe.wait_ge(S["stg_lo_first"], 2)
            pe.wait_ge(S["conv_sum_read"], 1)
            for n in range(2):
                out_part(1, 1, WO_ORDER[n], 4)
            for n in range(2, KC):
                if n < WO_EARLY:
                    pe.wait_ge(S["wo_lo_early"], n + 1)
                else:
                    pe.wait_ge(S["wo_lo"], n + 1 - WO_EARLY)
                for t in range(2):
                    for half in range(2):
                        ins = out_part(t, half, WO_ORDER[n], 4 * t)
                        if n == KC - 1:
                            ins.then_inc(S["out_done"], 1)
            for t in range(2, NT):
                pe.wait_ge(S["stg_lo"], t - 1)
                for half in range(2):
                    pe.wait_ge(S["x1_done"], half + 1 if t == 2 else 2 * t - 1 + half)
                    for k in WO_ORDER:
                        ins = out_part(t, half, k, 0)
                        if t == 3 and k == WO_ORDER[3]:
                            turn_h2(half)
                    ins.then_inc(S["out_done"], 1)
                if t >= 3:
                    turn_h2(t - 1)

            def gate_up(n, slot, half, first):
                for m, done in enumerate((S["gate_done"], S["up_done"])):
                    if not first:
                        if m == 0:
                            pe.wait_ge(S["silu_done"], 2 * n - 1 + half)
                        else:
                            pe.wait_ge(S["hid_done"], 2 * n - 1 + half)
                    product(ps[:, 2 * half + m, :], lambda a_, k: gu[slot][:, a_, m, k, :],
                            lambda b_, k: h[:, b_, k, half * HALF:(half + 1) * HALF], range(KC), True, True).then_inc(done, 1)
                    if first and half == 0:
                        if m == 1:
                            turn_h2(NT - 1)
                            pe.wait_ge(S["h2_lo"], NT)
                            pe.wait_ge(S["x1_squared"], NT)

            def down(g, first):
                pe.wait_ge(S["wd_lo"], 2 * g + 2)
                for t in range(NT):
                    if t % 4 == 0:
                        pe.wait_ge(S["act_lo"], 4 * g + 3 + t // 4)
                    for half in range(2):
                        m = 2 * t + half
                        if not (first and m < 4):
                            pe.wait_ge(S["res_added"], 2 * NT * g + m - 3)
                        product(ps[:, 4 + m % 4, :], lambda a_, cch: act[:, a_, cch, t * P:(t + 1) * P],
                                lambda b_, cch: wd[:, b_, cch, half * HALF:(half + 1) * HALF], range(2), True, True).then_inc(S["down_done"], 1)

            def ff(g, first):
                for slot in range(2):
                    pe.wait_ge(S["gu_lo"], 2 * g + slot + 1)
                    for half in range(2):
                        gate_up(2 * g + slot, slot, half, first and slot == 0)
                down(g, first)

            pe.wait_ge(S["h2_lo"], NT // 2)
            pe.wait_ge(S["x1_done"], 2 * NT)
            ff(0, True)
            with pe.Fori(1, FG) as g:
                ff(g, False)


def bucket_diagonals():
    import math
    import numpy as np
    table = np.zeros((BUCKETS + HQ, DIAGS), np.float32)
    exact = BUCKETS // 2
    for k in range(DIAGS):
        dist = 2 * P - 1 - k
        if 0 <= dist < WINDOW:
            b = dist if dist < exact else min(
                exact + int(math.log(dist / exact) / math.log(MAX_DISTANCE / exact) * (BUCKETS - exact)), BUCKETS - 1)
            table[b, k] = 1.0
        else:
            table[BUCKETS:, k] = MASKED
    return table


_INS = ["x", "c", "rel_bias", "w_ada", "b_ada", "g_norm1", "w_in", "sinks", "conv_w", "g_attn_out",
        "g_conv_out", "w_out", "g_norm2", "w_gu", "w_down", "g_final"]


def kernel(**inputs):
    import numpy as np
    import concourse.bacc as bacc
    from concourse.bass_utils import run_bass_kernel_spmd

    nc = bacc.Bacc("TRN2", target_bir_lowering=False, num_devices=1)
    arrays, args = {}, []
    for name in _INS + ["bucket_table"]:
        a = bucket_diagonals() if name == "bucket_table" else np.ascontiguousarray(inputs[name])
        if name not in ("rel_bias", "g_final", "bucket_table"):
            a = a.reshape(a.shape[1:])
        arrays[f"in_{name}"] = a
        args.append(nc.dram_tensor(f"in_{name}", a.shape, F32, kind="ExternalInput").ap())
    out = nc.dram_tensor("out_0", (SEQ, D), F32, kind="ExternalOutput").ap()
    hymba_layer(nc, *args, out)
    r = run_bass_kernel_spmd(nc, [arrays], core_ids=[0])
    return r.results[0]["out_0"].reshape(1, SEQ, D)
```
